# Optimizing a Trainium2 kernel written in Bass

```python
import math
import jax, jax.numpy as jnp
from jax import lax
import numpy as np

D_MODEL = 1024
BATCH = 1
SEQ = 512
DEPTH = 2

GRID_W = 64
CTX_LEN = 256
N_MIXERS = 4
KIND_POOL = 0
KIND_CONV = 1
KIND_MLA = 2
KIND_DIFF = 3
ATTN_KINDS = (KIND_MLA, KIND_DIFF)
Q_BLOCK = 128
ROPE_BASE = 10000.0
NORM_EPS = 1e-6
D_FF = 4 * D_MODEL
POOL_WINDOWS = (2, 4, 8, 16)
POOL_GROUP = D_MODEL // len(POOL_WINDOWS)
CONV_WIDTH = 3
MLA_HEADS = D_MODEL // 128
MLA_NOPE = 128
MLA_ROPE = 64
MLA_V = 128
MLA_Q_LORA = 3 * D_MODEL // 8
MLA_KV_LORA = D_MODEL // 4
MLA_SCALE = (MLA_NOPE + MLA_ROPE) ** -0.5
DIFF_HEADS = D_MODEL // 128
DIFF_HEAD_DIM = D_MODEL // (2 * DIFF_HEADS)
DIFF_SCALE = DIFF_HEAD_DIM ** -0.5

kernel_name = "hybrid_interleaved_diffusion_trunk"

def rms_norm(x, g):
    xf = x.astype(jnp.float32)
    y = xf * lax.rsqrt(jnp.mean(xf * xf, axis=-1, keepdims=True) + NORM_EPS)
    return (y * g.astype(jnp.float32)).astype(x.dtype)

def modulate(h, shift, scale):
    return h * (1.0 + scale) + shift

def axial_rope_tables(rows, rot_dim):
    t = jnp.arange(rows * GRID_W)
    row = (t // GRID_W).astype(jnp.float32)
    col = (t % GRID_W).astype(jnp.float32)
    n = rot_dim // 2
    inv_freq = ROPE_BASE ** (-jnp.arange(0, n, 2, dtype=jnp.float32) / n)

    def table(pos):
        ang = pos[:, None] * inv_freq[None, :]
        ang = jnp.concatenate([ang, ang], axis=-1)
        return (jnp.cos(ang), jnp.sin(ang))

    return table(row) + table(col)

def _rotate(x, cos, sin):
    half = x.shape[-1] // 2
    x1, x2 = x[..., :half], x[..., half:]
    return x * cos + jnp.concatenate([-x2, x1], axis=-1) * sin

def apply_axial_rope(x, rope):
    cos_r, sin_r, cos_c, sin_c = rope
    extra = x.ndim - 3

    def bc(t):
        return t.reshape((1, t.shape[0]) + (1,) * extra + (t.shape[1],))

    n = x.shape[-1] // 2
    xf = x.astype(jnp.float32)
    out = jnp.concatenate([_rotate(xf[..., :n], bc(cos_r), bc(sin_r)),
                           _rotate(xf[..., n:], bc(cos_c), bc(sin_c))], axis=-1)
    return out.astype(x.dtype)

def sweep_query_blocks(fn, *qs):
    b, length = qs[0].shape[:2]
    nb = length // Q_BLOCK
    blocks = tuple(jnp.moveaxis(q.reshape((b, nb, Q_BLOCK) + q.shape[2:]), 1, 0) for q in qs)
    out = lax.map(lambda blk: fn(*blk), blocks)
    return jnp.moveaxis(out, 0, 1).reshape((b, length) + out.shape[3:])

def pool_mixer(h, w_grp, scale):
    b, length, _ = h.shape
    hf = h.astype(jnp.float32)
    cs = jnp.concatenate([jnp.zeros_like(hf[:, :1]), jnp.cumsum(hf, axis=1)], axis=1)
    t = jnp.arange(length)
    parts = []
    for g, w in enumerate(POOL_WINDOWS):
        lo = w // 2
        hi = w - 1 - lo
        start = jnp.clip(t - lo, 0, length)
        end = jnp.clip(t + hi + 1, 0, length)
        sl = slice(g * POOL_GROUP, (g + 1) * POOL_GROUP)
        csg = cs[..., sl]
        win_sum = jnp.take(csg, end, axis=1) - jnp.take(csg, start, axis=1)
        count = (end - start).astype(jnp.float32)[None, :, None]
        parts.append(win_sum / count - hf[..., sl])
    d = jnp.stack(parts, axis=2).astype(h.dtype)
    y = jnp.einsum('blgc,gcd->blgd', d, w_grp).reshape(b, length, D_MODEL)
    return y * scale

def short_conv_mixer(h, w_in, conv_w, w_out):
    length = h.shape[1]
    b_gate, c_gate, v = jnp.split(h @ w_in, 3, axis=-1)
    u = c_gate * v
    pad = CONV_WIDTH // 2
    up = jnp.pad(u, ((0, 0), (pad, pad), (0, 0)))
    z = up[:, 0:length] * conv_w[0]
    for k in range(1, CONV_WIDTH):
        z = z + up[:, k:k + length] * conv_w[k]
    return (b_gate * z) @ w_out

def mla_mixer(h, hc, w_down, g_q, g_kv, w_uq, w_ukv, w_o, rope, need_ctx):
    def parse_q(a_q, rot):
        cq = rms_norm(a_q, g_q)
        q = (cq @ w_uq).reshape(a_q.shape[:2] + (MLA_HEADS, MLA_NOPE + MLA_ROPE))
        qn, qr = q[..., :MLA_NOPE], q[..., MLA_NOPE:]
        if rot is not None:
            qr = apply_axial_rope(qr, rot)
        return qn, qr

    def parse_kv(a_kv, rot):
        ckv = rms_norm(a_kv[..., :MLA_KV_LORA], g_kv)
        kr = a_kv[..., MLA_KV_LORA:]
        if rot is not None:
            kr = apply_axial_rope(kr, rot)
        kv = (ckv @ w_ukv).reshape(a_kv.shape[:2] + (MLA_HEADS, MLA_NOPE + MLA_V))
        return kv[..., :MLA_NOPE], kr, kv[..., MLA_NOPE:]

    def attend(qn, qr, kn, kr, v):
        def blk(qn_b, qr_b):
            s = (jnp.einsum('bqhd,bkhd->bhqk', qn_b, kn, preferred_element_type=jnp.float32)
                 + jnp.einsum('bqhr,bkr->bhqk', qr_b, kr, preferred_element_type=jnp.float32)) * MLA_SCALE
            p = jax.nn.softmax(s, axis=-1).astype(v.dtype)
            return jnp.einsum('bhqk,bkhd->bqhd', p, v)
        o = sweep_query_blocks(blk, qn, qr)
        return o.reshape(o.shape[:2] + (MLA_HEADS * MLA_V,)) @ w_o

    a = h @ w_down
    qn, qr = parse_q(a[..., :MLA_Q_LORA], rope)
    kn, kr, v = parse_kv(a[..., MLA_Q_LORA:], rope)
    if need_ctx:
        ac = hc @ w_down
        qn_c, qr_c = parse_q(ac[..., :MLA_Q_LORA], None)
        kn_c, kr_c, v_c = parse_kv(ac[..., MLA_Q_LORA:], None)
    else:
        kn_c, kr_c, v_c = parse_kv(hc @ w_down[:, MLA_Q_LORA:], None)
    y = attend(qn, qr, jnp.concatenate([kn, kn_c], axis=1), jnp.concatenate([kr, kr_c], axis=1),
               jnp.concatenate([v, v_c], axis=1))
    yc = attend(qn_c, qr_c, kn_c, kr_c, v_c) if need_ctx else None
    return y, yc

def diff_mixer(h, hc, w_qkv, lam_vecs, g_subln, w_o, lam_init, rope, need_ctx):
    lv = lam_vecs.astype(jnp.float32)
    lam = jnp.exp(jnp.sum(lv[0] * lv[1])) - jnp.exp(jnp.sum(lv[2] * lv[3])) + lam_init

    def heads_qk(t):
        return t.reshape(t.shape[:2] + (DIFF_HEADS, 2, DIFF_HEAD_DIM))

    def heads_v(t):
        return t.reshape(t.shape[:2] + (DIFF_HEADS, 2 * DIFF_HEAD_DIM))

    def attend(q, k, v):
        def blk(q_b):
            s = jnp.einsum('bqhjd,bkhjd->bhjqk', q_b, k, preferred_element_type=jnp.float32) * DIFF_SCALE
            p = jax.nn.softmax(s, axis=-1)
            a = p[:, :, 0] - lam * p[:, :, 1]
            return jnp.einsum('bhqk,bkhd->bqhd', a.astype(v.dtype), v)
        o = sweep_query_blocks(blk, q)
        o = rms_norm(o, g_subln) * (1.0 - lam_init)
        return o.reshape(o.shape[:2] + (D_MODEL,)) @ w_o

    q, k, v = jnp.split(h @ w_qkv, 3, axis=-1)
    q = apply_axial_rope(heads_qk(q), rope)
    k = apply_axial_rope(heads_qk(k), rope)
    v = heads_v(v)
    if need_ctx:
        qc, kc, vc = jnp.split(hc @ w_qkv, 3, axis=-1)
        qc = heads_qk(qc)
    else:
        kc, vc = jnp.split(hc @ w_qkv[:, D_MODEL:], 2, axis=-1)
    kc, vc = heads_qk(kc), heads_v(vc)
    y = attend(q, jnp.concatenate([k, kc], axis=1), jnp.concatenate([v, vc], axis=1))
    yc = attend(qc, kc, vc) if need_ctx else None
    return y, yc

def sqrelu_mlp(h, w1, w2):
    return jnp.square(jax.nn.relu(h @ w1)) @ w2

def setup_inputs(seed: int = 0) -> dict:
    key = jax.random.key(seed)
    k = jax.random.split(key, 24)

    def nrm(i, shape, scale):
        return jax.random.normal(k[i], shape, jnp.float32) * scale

    n_pool = len(range(KIND_POOL, DEPTH, N_MIXERS))
    n_conv = len(range(KIND_CONV, DEPTH, N_MIXERS))
    n_mla = len(range(KIND_MLA, DEPTH, N_MIXERS))
    n_diff = len(range(KIND_DIFF, DEPTH, N_MIXERS))
    D = D_MODEL
    return dict(
        x=nrm(0, (BATCH, SEQ, D), 1.0),
        c=nrm(1, (BATCH, D), 1.0),
        ctx=nrm(2, (BATCH, CTX_LEN, D), 1.0),
        c_ctx=nrm(3, (D,), 1.0),
        ada_w=nrm(4, (DEPTH, D, 6 * D), 0.5 * D ** -0.5),
        ada_b=nrm(5, (DEPTH, 6 * D), 0.02),
        norm_g=1.0 + nrm(6, (DEPTH, 4, D), 0.05),
        ffn_w1=nrm(7, (DEPTH, D, D_FF), D ** -0.5),
        ffn_w2=nrm(8, (DEPTH, D_FF, D), D_FF ** -0.5),
        pool_w=nrm(9, (n_pool, len(POOL_WINDOWS), POOL_GROUP, POOL_GROUP), POOL_GROUP ** -0.5),
        pool_scale=1.0 + nrm(10, (n_pool, D), 0.1),
        conv_in_w=nrm(11, (n_conv, D, 3 * D), D ** -0.5),
        conv_w=nrm(12, (n_conv, CONV_WIDTH, D), CONV_WIDTH ** -0.5),
        conv_out_w=nrm(13, (n_conv, D, D), D ** -0.5),
        mla_w_down=nrm(14, (n_mla, D, MLA_Q_LORA + MLA_KV_LORA + MLA_ROPE), D ** -0.5),
        mla_g_q=1.0 + nrm(15, (n_mla, MLA_Q_LORA), 0.05),
        mla_g_kv=1.0 + nrm(16, (n_mla, MLA_KV_LORA), 0.05),
        mla_w_uq=nrm(17, (n_mla, MLA_Q_LORA, MLA_HEADS * (MLA_NOPE + MLA_ROPE)), MLA_Q_LORA ** -0.5),
        mla_w_ukv=nrm(18, (n_mla, MLA_KV_LORA, MLA_HEADS * (MLA_NOPE + MLA_V)), MLA_KV_LORA ** -0.5),
        mla_w_o=nrm(19, (n_mla, MLA_HEADS * MLA_V, D), (MLA_HEADS * MLA_V) ** -0.5),
        diff_w_qkv=nrm(20, (n_diff, D, 3 * D), D ** -0.5),
        diff_lambda=nrm(21, (n_diff, 4, DIFF_HEAD_DIM), 0.1),
        diff_g_subln=1.0 + nrm(22, (n_diff, 2 * DIFF_HEAD_DIM), 0.05),
        diff_w_o=nrm(23, (n_diff, D, D), D ** -0.5),
    )

def reference(x, c, ctx, c_ctx, ada_w, ada_b, norm_g, ffn_w1, ffn_w2, pool_w, pool_scale,
              conv_in_w, conv_w, conv_out_w, mla_w_down, mla_g_q, mla_g_kv, mla_w_uq, mla_w_ukv,
              mla_w_o, diff_w_qkv, diff_lambda, diff_g_subln, diff_w_o):
    rows = x.shape[1] // GRID_W
    rope_mla = axial_rope_tables(rows, MLA_ROPE)
    rope_diff = axial_rope_tables(rows, DIFF_HEAD_DIM)
    silu_c = jax.nn.silu(c)
    silu_cc = jax.nn.silu(c_ctx)
    xc = ctx
    for i in range(DEPTH):
        kind = i % N_MIXERS
        j = i // N_MIXERS
        ctx_out = i < DEPTH - 1
        ctx_in = ctx_out or kind in ATTN_KINDS
        sh_m, sc_m, gt_m, sh_f, sc_f, gt_f = jnp.split(
            (silu_c @ ada_w[i] + ada_b[i])[:, None, :], 6, axis=-1)
        h = modulate(rms_norm(x, norm_g[i, 0]), sh_m, sc_m)
        hc = None
        if ctx_in:
            mc = jnp.split(silu_cc @ ada_w[i] + ada_b[i], 6)
            hc = modulate(rms_norm(xc, norm_g[i, 0]), mc[0], mc[1])
        if kind == KIND_POOL:
            y = pool_mixer(h, pool_w[j], pool_scale[j])
            yc = pool_mixer(hc, pool_w[j], pool_scale[j]) if ctx_out else None
        elif kind == KIND_CONV:
            y = short_conv_mixer(h, conv_in_w[j], conv_w[j], conv_out_w[j])
            yc = short_conv_mixer(hc, conv_in_w[j], conv_w[j], conv_out_w[j]) if ctx_out else None
        elif kind == KIND_MLA:
            y, yc = mla_mixer(h, hc, mla_w_down[j], mla_g_q[j], mla_g_kv[j], mla_w_uq[j],
                              mla_w_ukv[j], mla_w_o[j], rope_mla, ctx_out)
        else:
            lam_init = 0.8 - 0.6 * math.exp(-0.3 * i)
            y, yc = diff_mixer(h, hc, diff_w_qkv[j], diff_lambda[j], diff_g_subln[j], diff_w_o[j],
                               lam_init, rope_diff, ctx_out)
        x = x + gt_m * rms_norm(y, norm_g[i, 1])
        hf = modulate(rms_norm(x, norm_g[i, 2]), sh_f, sc_f)
        x = x + gt_f * rms_norm(sqrelu_mlp(hf, ffn_w1[i], ffn_w2[i]), norm_g[i, 3])
        if ctx_out:
            xc = xc + mc[2] * rms_norm(yc, norm_g[i, 1])
            hcf = modulate(rms_norm(xc, norm_g[i, 2]), mc[3], mc[4])
            xc = xc + mc[5] * rms_norm(sqrelu_mlp(hcf, ffn_w1[i], ffn_w2[i]), norm_g[i, 3])
    return x


_drawn_inputs = setup_inputs


def setup_inputs(seed=0):
    import zlib

    import numpy as np

    out = dict(_drawn_inputs(seed))
    spreads = {}
    factors = {}
    for name, (base, spread) in spreads.items():
        noise = np.random.default_rng([zlib.crc32(name.encode()), seed]).standard_normal(out[name].shape)
        drawn = base * np.exp(spread * noise) if base else spread * noise
        out[name] = __import__('jax').numpy.asarray(drawn.astype(out[name].dtype))
    for name, factor in factors.items():
        out[name] = (out[name] * factor).astype(out[name].dtype)
    return out
```

```python
from contextlib import ExitStack

import concourse.bass as bass
from concourse import mybir

F32 = mybir.dt.float32
F32R = mybir.dt.float32r
ALU = mybir.AluOpType
ACT = mybir.ActivationFunctionType

P = 128
D = 1024
NC = D // P
T = 512
NT = T // P
FF = 4096
EPS = 1e-6
WINDOWS = (2, 4, 8, 16)
GROUP = D // len(WINDOWS)
PAD = max(WINDOWS) // 2
LEVEL = T + 2 * PAD

UK, UN = 4, 512
BANKS = UN // P
QUARTERS = 4
QF = FF // QUARTERS
Q_UNITS = 8
POOL_U = 0
FFN_U = (1, 1 + 4 * Q_UNITS + 16)
CONV_U = 1 + 4 * Q_UNITS
OUT_U = CONV_U + 12
UNITS = FFN_U[1] + 4 * Q_UNITS
RAW_SLOTS = 2
CV_GROUPS = (0, 1, 3, 4)
CV_COLS = (0, 256, 128, 384)

SHIFT_M, SCALE_M, GATE_M, SHIFT_F, SCALE_F, GATE_F = range(6)
FIRST_SEGS = (SCALE_M, SHIFT_M, GATE_M, SCALE_F, SHIFT_F)
LATER_SEGS = 7
ADA_SLOTS = 4
ADA_FIRST = len(FIRST_SEGS) * NC
ADA_Q = 2 * LATER_SEGS

V_ADA_B = 0
V_NORM_G = 2 * 6 * NC
V_POOL = V_NORM_G + 2 * 4 * NC
V_CONV = V_POOL + NC
V_C = V_CONV + 3 * NC
V_END = V_C + NC

POOL_BANK = (0, 1, 2, 3, 4, 7, 0, 1)
BCAST_BANK, STAT_BANK = 6, 7


def trunk(nc, x, c, ada_w, ada_b, norm_g, ffn_w1, ffn_w2, pool_w, pool_scale, conv_in_w, conv_w, conv_out_w, out):
    with ExitStack() as ctx:
        def sb(name, shape, dt=F32):
            return ctx.enter_context(nc.sbuf_tensor(name, shape, dt))

        def sem(name):
            return ctx.enter_context(nc.semaphore(name))

        xs = sb("xs", [P, NC, T])
        in_hi = sb("in_hi", [P, NC, T], F32R)
        in_lo = sb("in_lo", [P, NC, T], F32R)
        mid_hi = sb("mid_hi", [P, NC, T], F32R)
        mid_lo = sb("mid_lo", [P, NC, T], F32R)
        y = sb("y", [P, NC, T])
        raw = sb("raw", [P, RAW_SLOTS, UK * UN])
        w_hi = sb("w_hi", [P, 2, UK * UN], F32R)
        w_lo = sb("w_lo", [P, 2, UK * UN], F32R)
        ada_raw = sb("ada_raw", [P, ADA_SLOTS, D])
        ada_sum = sb("ada_sum", [P, LATER_SEGS, D])
        relu = sb("relu", [P, 2, LEVEL])
        sq = sb("sq", [P, 2, LEVEL])
        ssq = sb("ssq", [P, T])
        diag = sb("diag", [P, NT, P])
        vec_rows = sb("vec_rows", [P, 2, P])
        vec = sb("vec", [P, V_END])
        mod = sb("mod", [P, 2, 6, NC])
        mod_t = sb("mod_t", [P, 2, 6, NC])
        silu_t = sb("silu_t", [P, 4, NC])
        std = sb("std", [P, 2, NT])
        edge = sb("edge", [P, 2, 32])
        ident = sb("ident", [P, P])
        ones = sb("ones", [P, P])
        eps = sb("eps", [P, 1])
        ps = ctx.enter_context(nc.psum_tensor("ps", [P, 8, T], F32))

        x_tok = raw[:, :, :].rearrange("p s (j d) -> p (s j) d", d=D)
        norm0 = ada_sum[:, 5:7, :].rearrange("p s (a t) -> p (s a) t", a=2)
        flat = ada_sum[:, :, :].rearrange("p s d -> p (s d)")
        cgate = flat[:, 0:2 * T].rearrange("p (s t) -> p s t", s=2)
        cu = flat[:, 2 * T:2 * T + 2 * (T + 2)].rearrange("p (s t) -> p s t", s=2)


        x_in, vec_in, out_done = sem("x_in"), sem("vec_in"), sem("out_done")
        raw_in = [sem(f"raw_in{s}") for s in range(RAW_SLOTS)]
        ada_in = [sem(f"ada_in{s}") for s in range(ADA_SLOTS)]
        consts_ready, ident_zero, eps_ready = sem("consts_ready"), sem("ident_zero"), sem("eps_ready")
        vec_turned, vec_ready = sem("vec_turned"), sem("vec_ready")
        exp_ready, silu_step = sem("exp_ready"), sem("silu_step")
        x_turned, x_copied = sem("x_turned"), sem("x_copied")
        w_hi_ready, w_lo_ready = sem("w_hi_ready"), sem("w_lo_ready")
        unit_done, bank_done = sem("unit_done"), sem("bank_done")
        ada_used, ada_cols, mod_step, mod_ready, sums_zero = sem("ada_used"), sem("ada_cols"), sem("mod_step"), sem("mod_ready"), sem("sums_zero")
        norm0_ready, level_step, window_ready = sem("norm0_ready"), sem("level_step"), sem("window_ready")
        pool_t, pool_mean, pool_h, pool_diff = sem("pool_t"), sem("pool_mean"), sem("pool_h"), sem("pool_diff")
        relu_done, hid_hi, hid_sq, hid_lo = sem("relu_done"), sem("hid_hi"), sem("hid_sq"), sem("hid_lo")
        y_zero, y_sum, y_copied, y_sq, ssq_step = sem("y_zero"), sem("y_sum"), sem("y_copied"), sem("y_sq"), sem("ssq_step")
        x_sq, x_stat = sem("x_sq"), sem("x_stat")
        cols_done, std_done, rs_done, diag_done, bcast_done = (sem("cols_done"), sem("std_done"), sem("rs_done"),
                                                               sem("diag_done"), sem("bcast_done"))
        y_norm, x_new = sem("y_norm"), sem("x_new")
        h_norm, h_full, h_hi, h_lo = sem("h_norm"), sem("h_full"), sem("h_hi"), sem("h_lo")
        c_copied, cu_ready, cu_pad = sem("c_copied"), sem("cu_ready"), sem("cu_pad")
        z_mid, z_left, z_ready = sem("z_mid"), sem("z_left"), sem("z_ready")
        gated, g_hi, g_lo = sem("gated"), sem("g_hi"), sem("g_lo")
        out_turned, out_by_act, out_by_dve = sem("out_turned"), sem("out_by_act"), sem("out_by_dve")

        block = ctx.enter_context(nc.Block())

        def pair(u):
            return (u - 1) // 2

        def unit_wait(eng, first, pairs):
            if first:
                eng.wait_ge(unit_done, pairs + 1)
            else:
                eng.wait_ge(bank_done, NC + BANKS * (pairs + 1))

        def raw_value(u):
            n = 0
            for v in range(u % 2, u + 1, 2):
                n += 32 if CONV_U <= v < OUT_U and (v - CONV_U) // 2 in CV_GROUPS else 16
            return n

        def col(base, chunk):
            return vec[:, base + chunk:base + chunk + 1]

        GATES = ((0, 2), (0, 5), (1, 2), (1, 5))
        INPUTS = ((0, 3), (1, 0), (1, 3))
        GATE_MODS = (5, 6, 9, 12)
        INPUT_MODS = (5, 8, 11)
        LATER = {1: ((0,), (1, 2)), 2: ((3,), (4, 5)), 3: ((6,), ())}

        def raw_cols(slot, cols=slice(0, UN)):
            return raw[:, slot, :].rearrange("p (k n) -> p k n", k=UK)[:, :, cols]

        def w_rows(w):
            return w.rearrange("(k p) n -> p k n", p=P)

        @block.sync
        def _(sp):
            sp.dma_start(x_tok, x[0].rearrange("(j p) d -> p j d", p=P)).then_inc(x_in, 16)

            def load_ada(a):
                if a >= ADA_SLOTS:
                    sp.wait_ge(ada_used, a - ADA_SLOTS + 1)
                seg, k = FIRST_SEGS[a // NC], a % NC
                sp.dma_start(ada_raw[:, a % ADA_SLOTS, :],
                             ada_w[0, k * P:(k + 1) * P, seg * D:(seg + 1) * D]).then_inc(ada_in[a % ADA_SLOTS], 16)

            def load_mlp(layer):
                with sp.Fori(0, QUARTERS) as q:
                    for j in range(Q_UNITS):
                        u = FFN_U[layer] + j
                        sp.wait_ge(w_lo_ready, q * Q_UNITS + max(u - 1, 1))
                        if j < 4:
                            src = ffn_w1[layer, (j % 2) * UK * P:(j % 2 + 1) * UK * P,
                                         bass.ds(q * QF + (j // 2) * UN, UN)]
                        else:
                            src = ffn_w2[layer, bass.ds(q * QF + (j % 2) * UK * P, UK * P),
                                         (j // 2 - 2) * UN:(j // 2 - 1) * UN]
                        sp.dma_start(raw_cols(u % 2), w_rows(src)).then_inc(raw_in[u % 2], 16)

            for a in range(2 * NC):
                load_ada(a)
            sp.wait_ge(x_turned, NC)
            sp.dma_start(raw[:, 0, :].rearrange("p (g n) -> p g n", g=2 * len(WINDOWS)),
                         pool_w[0].rearrange("g (k p) n -> p (g k) n", p=P)).then_inc(raw_in[0], 16)
            for a in range(2 * NC, ADA_FIRST):
                load_ada(a)
            load_mlp(0)
            for u in range(CONV_U, FFN_U[1]):
                sp.wait_ge(w_lo_ready, u - 1)
                if u < OUT_U:
                    g, kk = (u - CONV_U) // 2, (u - CONV_U) % 2
                    rows = conv_in_w[0, kk * UK * P:(kk + 1) * UK * P, :]
                    if g in CV_GROUPS:
                        n = CV_GROUPS.index(g) * UN // 2
                        for i in (0, 1):
                            sp.dma_start(raw_cols(u % 2, slice(i * UN // 2, (i + 1) * UN // 2)),
                                         w_rows(rows[:, (1 + i) * D + n:(1 + i) * D + n + UN // 2])).then_inc(raw_in[u % 2], 16)
                    else:
                        n = (g // 3) * UN
                        sp.dma_start(raw_cols(u % 2), w_rows(rows[:, n:n + UN])).then_inc(raw_in[u % 2], 16)
                else:
                    g, kk = (u - OUT_U) // 2, (u - OUT_U) % 2
                    sp.dma_start(raw_cols(u % 2), w_rows(conv_out_w[0, kk * UK * P:(kk + 1) * UK * P,
                                                                    g * UN:(g + 1) * UN])).then_inc(raw_in[u % 2], 16)
            load_mlp(1)
            for half in range(2):
                for j in range(NT):
                    if half == 1 and j >= 2:
                        sp.wait_ge(out_by_dve, j - 1)
                    else:
                        sp.wait_ge(out_by_act, half * NT + j + 1)
                    sp.dma_start(out[0, j * P:(j + 1) * P, half * T:(half + 1) * T],
                                 x_tok[:, j, half * T:(half + 1) * T]).then_inc(out_done, 16)
            sp.wait_ge(out_done, 16 * 2 * NT)

        @block.tensor
        def _(pe):
            def multiply(u, q, hi, lo, chunks, need, banks=None, cols=None):
                first = (u - 1) % 2 == 0
                banks = banks or [BANKS * (pair(u) % 2) + m for m in range(BANKS)]
                cols = cols or [m * P for m in range(BANKS)]
                pe.wait_ge(w_lo_ready, q * Q_UNITS + (u + 1))

                def products(kk, m):
                    n = kk * UN + cols[m]
                    a, b = w_hi[:, u % 2, n:n + P], w_lo[:, u % 2, n:n + P]
                    o = ps[:, banks[m], :]
                    nc.tensor.matmul(o, a, hi[:, chunks[kk], :], start=first and kk == 0, stop=False)
                    nc.tensor.matmul(o, a, lo[:, chunks[kk], :], start=False, stop=False)
                    return nc.tensor.matmul(o, b, hi[:, chunks[kk], :], start=False, stop=not first and kk == UK - 1)

                if first:
                    for kk in range(UK):
                        need(kk)
                        for m in range(BANKS):
                            last = products(kk, m)
                    last.then_inc(unit_done, 1)
                else:
                    need(UK - 1)
                    for m in range(BANKS):
                        for kk in range(UK):
                            last = products(kk, m)
                        last.then_inc(bank_done, 1)

            def mlp(layer):
                ready = NC * (2 + 2 * layer)
                with pe.Fori(0, QUARTERS) as q:
                    for j in range(Q_UNITS):
                        u = FFN_U[layer] + j
                        half = UK * (j % 2)
                        chunks = [half + kk for kk in range(UK)]
                        if j < 4:
                            multiply(u, q, in_hi, in_lo, chunks,
                                     lambda kk, n=ready - NC + half: pe.wait_ge(h_lo, n + kk + 1))
                        else:
                            multiply(u, q, mid_hi, mid_lo, chunks,
                                     lambda kk, n=layer * QUARTERS * NC + half: pe.wait_ge(hid_lo, q * NC + (n + kk + 1)))

            def stat_cols(at, src, first, last):
                for j in range(NT):
                    mm = nc.tensor.matmul(ps[:, STAT_BANK, at + j:at + j + 1], src[:, j * P:(j + 1) * P], ones[:, 0:1],
                                          start=first and j == 0, stop=last, skip_group_check=True)
                return mm

            def broadcast(k):
                pe.wait_ge(diag_done, k + 1)
                nc.tensor.matmul(ps[:, BCAST_BANK, :], ones[:, :], diag[:, :, :], start=True, stop=True).then_inc(bcast_done, 1)

            def reduce_sum(s, bank, at):
                for m in range(NC):
                    mm = nc.tensor.matmul(ps[:, bank, at + m:at + m + 1], ada_sum[:, s, m * P:(m + 1) * P], ones[:, 0:1],
                                          start=True, stop=True)
                mm.then_inc(ada_cols, 1)

            def x_stats(b, n):
                pe.wait_ge(x_sq, NC * (b + 1) + n + 1)
                stat_cols(8, sq[:, n % 2, 0:T], n == 0, n == NC - 1).then_inc(x_stat, 1)

            def boundary(b):
                gates, inputs = LATER.get(b, ((), ()))
                if gates:
                    pe.wait_ge(ada_used, ADA_FIRST + QUARTERS * ADA_Q)
                    pe.wait_ge(y_sq, NC * b + 4)
                for s in gates:
                    reduce_sum(s, 0, 0)
                pe.wait_ge(ssq_step, (NC - 1) * (b + 1))
                stat_cols(0, ssq, True, True).then_inc(cols_done, 1)
                broadcast(2 * b + 1)
                for i, s in enumerate(inputs):
                    reduce_sum(s, 1, 8 * i)
                if b < 3:
                    for n in range(NC):
                        x_stats(b, n)
                    broadcast(2 * b + 2)
                else:
                    for n in range(NC):
                        pe.wait_ge(x_new, NC * 3 + n + 1)
                        if n == 4:
                            pe.wait_ge(out_by_act, NT)
                        for j in range(NT):
                            tr = nc.tensor.transpose(ps[:, j, (n % 4) * P:(n % 4 + 1) * P], xs[:, n, j * P:(j + 1) * P], ident[:, :])
                        tr.then_inc(out_turned, 1)

            pe.wait_ge(consts_ready, 2)
            pe.wait_ge(vec_in, 16 * 5)
            for s, (n, at) in enumerate(((V_NORM_G, 0), (V_END - V_NORM_G, V_NORM_G))):
                tr = nc.tensor.transpose(ps[:, 5, at:at + n], vec_rows[0:n, s, :], ident[0:n, 0:n])
            tr.then_inc(vec_turned, 1)
            pe.wait_ge(x_in, 16)
            for n in range(NC):
                if n >= 2:
                    x_stats(-1, n - 2)
                for j in range(NT):
                    tr = nc.tensor.transpose(ps[:, n % 4, j * P:(j + 1) * P], x_tok[:, j, n * P:(n + 1) * P], ident[:, :])
                tr.then_inc(x_turned, 1)
            x_stats(-1, NC - 2)
            x_stats(-1, NC - 1)
            broadcast(0)
            for s in range(2):
                pe.wait_ge(ada_used, NC * (s + 1))
                reduce_sum(s, 4 + s, 0)

            def pool_group(g):
                for n in (2 * g, 2 * g + 1):
                    if n >= 6:
                        pe.wait_ge(y_sq, n - 5)
                    for kk in range(2):
                        pe.wait_ge(h_lo, 2 * g + kk + 1)
                        at = (2 * g + kk) * GROUP + (n % 2) * P
                        a, b = w_hi[:, 0, at:at + P], w_lo[:, 0, at:at + P]
                        o = ps[:, POOL_BANK[n], :]
                        nc.tensor.matmul(o, a, in_hi[:, 2 * g + kk, :], start=kk == 0, stop=False)
                        nc.tensor.matmul(o, a, in_lo[:, 2 * g + kk, :], start=False, stop=False)
                        mm = nc.tensor.matmul(o, b, in_hi[:, 2 * g + kk, :], start=False, stop=kk == 1)
                    mm.then_inc(bank_done, 1)

            pe.wait_ge(w_lo_ready, 1)
            for g in range(len(WINDOWS)):
                pool_group(g)
            for s in range(2, len(FIRST_SEGS)):
                pe.wait_ge(ada_used, NC * (s + 1))
                reduce_sum(s, 5, 8 * (s - 2))
            boundary(0)
            mlp(0)
            boundary(1)
            for g in range(6):
                for kk in (0, 1):
                    multiply(CONV_U + 2 * g + kk, 0, in_hi, in_lo, [UK * kk + i for i in range(UK)],
                             lambda i, n=NC * 2 + UK * kk: pe.wait_ge(h_lo, n + i + 1),
                             cols=CV_COLS if g in CV_GROUPS else None)
            for g in range(2):
                for kk in (0, 1):
                    multiply(OUT_U + 2 * g + kk, 0, mid_hi, mid_lo, [UK * kk + i for i in range(UK)],
                             lambda i, n=UK * kk: pe.wait_ge(g_lo, n + i + 1))
            boundary(2)
            mlp(1)
            boundary(3)

        @block.scalar
        def _(act):
            def split_hi(u, q=0):
                raw_at = raw_value(u + Q_UNITS * q) if isinstance(q, int) else q * (16 * Q_UNITS // 2) + raw_value(u)
                act.wait_ge(raw_in[u % 2], raw_at)
                if u == 2:
                    act.wait_ge(bank_done, NC)
                elif u > 2:
                    unit_wait(act, (u - 3) % 2 == 0, q * (Q_UNITS // 2) + pair(u - 2))
                nc.scalar.activation(w_hi[:, u % 2, :], raw[:, u % 2, :], ACT.Copy).then_inc(w_hi_ready, 1)

            def y_square(b, n, src):
                if n >= 3:
                    act.wait_ge(ssq_step, (NC - 1) * b + n - 2)
                nc.scalar.activation(ssq[:, :] if n == 0 else sq[:, n % 2, 0:T], src, ACT.Square).then_inc(y_sq, 1)

            def root(k):
                act.wait_ge(cols_done if k % 2 else x_stat, k // 2 + 1 if k % 2 else NC * (k // 2 + 1))
                at = 0 if k % 2 else 8
                nc.scalar.activation(std[:, 0, :], ps[:, STAT_BANK, at:at + NT], ACT.Sqrt, bias=eps[:, 0:1],
                                     scale=1.0 / D).then_inc(std_done, 1)

            def load_ada(q, j):
                for i in (2 * j, 2 * j + 1):
                    act.wait_ge(ada_used, q * ADA_Q + (ADA_FIRST - 1 + i))
                    seg, kk = i % LATER_SEGS, i // LATER_SEGS
                    rows = bass.ds(q * 2 * P + kk * P, P)
                    src = (ada_w[0, rows, GATE_F * D:(GATE_F + 1) * D] if seg == 0 else
                           ada_w[1, rows, (seg - 1) * D:seg * D])
                    act.dma_start(ada_raw[:, i % 2, :], src).then_inc(ada_in[i % 2], 16)

            def mlp_quarter(layer, q, last=False):
                b = 1 + 2 * layer
                for j in range(Q_UNITS):
                    u = FFN_U[layer] + j
                    if j in (1, 3):
                        for m in range(BANKS):
                            n = BANKS * (j // 2) + m
                            i = layer * QUARTERS * NC + n
                            group = NC + BANKS * pair(u) + m + 1
                            act.wait_ge(bank_done, q * (BANKS * Q_UNITS // 2) + group)
                            if n >= 2 or i - n > 0:
                                act.wait_ge(hid_lo, q * NC + (i - 1))
                            nc.scalar.activation(relu[:, n % 2, 0:T], ps[:, BANKS * (j // 2) + m, :], ACT.Relu).then_inc(relu_done, 1)
                            act.wait_ge(relu_done, q * NC + (i + 1))
                            nc.scalar.activation(mid_hi[:, n, :], relu[:, n % 2, 0:T], ACT.Square).then_inc(hid_hi, 1)
                    if last and j in (5, 7):
                        for m in range(BANKS):
                            n = BANKS * (j // 2 - 2) + m
                            act.wait_ge(y_sum, NC * (QUARTERS * (layer + 1) - 1) + n + 1)
                            y_square(b, n, y[:, n, :])
                    if not (last and u + Q_UNITS * q + 2 >= UNITS):
                        split_hi(u + 2, q)
                    if layer == 0 and j + 1 < LATER_SEGS:
                        load_ada(q, j + 1)
                    if layer == 0 and j + 1 == Q_UNITS and not last:
                        load_ada(q + 1, 0)

            def boundary(b):
                root(2 * b + 1)
                if b == 3:
                    for half in range(2):
                        for j in range(NT - 2 * half):
                            act.wait_ge(out_turned, 4 * (half + 1))
                            nc.scalar.activation(x_tok[:, j, half * T:(half + 1) * T], ps[:, j, :], ACT.Copy).then_inc(out_by_act, 1)
                    return
                for n in range(NC):
                    act.wait_ge(x_new, NC * b + n + 1)
                    if n >= 2:
                        act.wait_ge(x_stat, NC * (b + 1) + n - 1)
                    nc.scalar.activation(sq[:, n % 2, 0:T], xs[:, n, :], ACT.Square).then_inc(x_sq, 1)
                root(2 * b + 2)
                for n in range(NC):
                    act.wait_ge(h_full, NC * b + n + 1)
                    nc.scalar.activation(in_hi[:, n, :], y[:, n, :], ACT.Copy).then_inc(h_hi, 1)

            act.dma_start(vec_rows[0:V_NORM_G, 0, :], ada_b.rearrange("l (r p) -> (l r) p", p=P)).then_inc(vec_in, 16)
            at = 0
            for v, n in ((norm_g.rearrange("l g (r p) -> (l g r) p", p=P), V_POOL - V_NORM_G),
                         (pool_scale.rearrange("l (r p) -> (l r) p", p=P), NC),
                         (conv_w.rearrange("l w (r p) -> (l w r) p", p=P), 3 * NC),
                         (c.rearrange("l (r p) -> (l r) p", p=P), NC)):
                act.dma_start(vec_rows[at:at + n, 1, :], v).then_inc(vec_in, 16)
                at += n
            act.wait_ge(vec_turned, 1)
            nc.scalar.activation(vec[:, :], ps[:, 5, 0:V_END], ACT.Copy).then_inc(vec_ready, 1)
            act.wait_ge(vec_ready, 1)
            nc.scalar.activation(silu_t[:, 0, :], vec[:, V_C:V_END], ACT.Exp, scale=-1.0).then_inc(exp_ready, 1)
            for n in range(NC):
                act.wait_ge(x_turned, n + 1)
                nc.scalar.activation(xs[:, n, :], ps[:, n % 4, :], ACT.Copy).then_inc(x_copied, 1)
                if n >= 2:
                    act.wait_ge(x_stat, n - 1)
                nc.scalar.activation(sq[:, n % 2, 0:T], ps[:, n % 4, :], ACT.Square).then_inc(x_sq, 1)
            act.wait_ge(eps_ready, 1)
            root(0)
            split_hi(POOL_U)
            for n in range(NC):
                A, B = mod[:, 0, 0, n:n + 1], mod[:, 0, 1, n:n + 1]
                act.wait_ge(mod_ready, 2)
                act.wait_ge(window_ready, n // 2 + 1)
                nc.scalar.activation(y[:, n, :], y[:, n, :], ACT.Identity, bias=B, scale=A).then_inc(pool_mean, 1)
                act.wait_ge(pool_t, n + 1)
                nc.scalar.activation(norm0[:, n % 4, :], norm0[:, n % 4, :], ACT.Identity, bias=B, scale=A).then_inc(pool_h, 1)
                if n >= 1:
                    act.wait_ge(pool_diff, n)
                    nc.scalar.activation(in_hi[:, n - 1, :], y[:, n - 1, :], ACT.Copy).then_inc(h_hi, 1)
            act.wait_ge(pool_diff, NC)
            nc.scalar.activation(in_hi[:, NC - 1, :], y[:, NC - 1, :], ACT.Copy).then_inc(h_hi, 1)
            for n in range(NC):
                act.wait_ge(bank_done, n + 1)
                nc.scalar.activation(y[:, n, :], ps[:, POOL_BANK[n], :], ACT.Copy, scale=col(V_POOL, n)).then_inc(y_copied, 1)
                act.wait_ge(y_copied, n + 1)
                y_square(0, n, y[:, n, :])
            split_hi(1)
            split_hi(2)
            load_ada(0, 0)
            boundary(0)
            with act.Fori(0, QUARTERS - 1) as q:
                mlp_quarter(0, q)
            mlp_quarter(0, QUARTERS - 1, last=True)
            boundary(1)
            for g in range(6):
                u = CONV_U + 2 * g
                split_hi(u + 2)
                if g in CV_GROUPS:
                    for p in (0, 1):
                        n = 2 * CV_GROUPS.index(g) + p
                        act.wait_ge(bank_done, NC + BANKS * pair(u) + 2 * p + 1)
                        if n >= 2:
                            act.wait_ge(cu_ready, n - 1)
                        nc.scalar.activation(cgate[:, p, :], ps[:, BANKS * (g % 2) + 2 * p, :], ACT.Copy).then_inc(c_copied, 1)
                        act.wait_ge(cu_ready, n + 1)
                        nc.scalar.activation(y[:, n, :], cu[:, p, 1:T + 1], ACT.Copy, scale=col(V_CONV + NC, n)).then_inc(z_mid, 1)
                else:
                    for m in range(BANKS):
                        n = BANKS * (g // 3) + m
                        act.wait_ge(gated, n + 1)
                        nc.scalar.activation(mid_hi[:, n, :], y[:, n, :], ACT.Copy).then_inc(g_hi, 1)
                split_hi(u + 3)
            for g in range(2):
                u = OUT_U + 2 * g
                split_hi(u + 2)
                for m in range(BANKS):
                    n = BANKS * g + m
                    act.wait_ge(bank_done, NC + BANKS * pair(u) + m + 1)
                    nc.scalar.activation(y[:, n, :], ps[:, BANKS * g + m, :], ACT.Copy).then_inc(y_copied, 1)
                    y_square(2, n, ps[:, BANKS * g + m, :])
                split_hi(u + 3)
            boundary(2)
            with act.Fori(0, QUARTERS - 1) as q:
                mlp_quarter(1, q)
            mlp_quarter(1, QUARTERS - 1, last=True)
            boundary(3)

        @block.vector
        def _(dve):
            def split_lo(u, q=0):
                dve.wait_ge(w_hi_ready, q * Q_UNITS + (u + 1))
                nc.vector.tensor_tensor(w_lo[:, u % 2, :], raw[:, u % 2, :], w_hi[:, u % 2, :].bitcast(F32), ALU.subtract).then_inc(w_lo_ready, 1)

            def add_ada(a, slot, landed, s, c_col, start):
                dve.wait_ge(ada_in[slot], landed)
                if start:
                    nc.vector.tensor_scalar(ada_sum[:, s, :], ada_raw[:, slot, :], c_col, None, ALU.mult).then_inc(ada_used, 1)
                else:
                    nc.vector.scalar_tensor_tensor(out=ada_sum[:, s, :], in0=ada_raw[:, slot, :], scalar=c_col,
                                                   in1=ada_sum[:, s, :], op0=ALU.mult, op1=ALU.add).then_inc(ada_used, 1)

            def first_ada(a):
                s, k = a // NC, a % NC
                if k:
                    dve.wait_ge(ada_used, a)
                add_ada(a, a % ADA_SLOTS, 16 * (a // ADA_SLOTS + 1), s, silu_t[:, 3, k:k + 1], k == 0)

            def make_mod(i, layer, seg, bank, at):
                dve.wait_ge(ada_cols, i)
                src = ps[:, bank, at:at + NC]
                bias = vec[:, V_ADA_B + (layer * 6 + seg) * NC:V_ADA_B + (layer * 6 + seg + 1) * NC]
                mlp = seg >= SHIFT_F
                if seg in (SHIFT_M, SHIFT_F):
                    nc.vector.tensor_tensor(mod[:, layer, 3 * mlp + 1, :], src, bias, ALU.add).then_inc(mod_ready, 1)
                    return
                nc.vector.tensor_tensor(mod_t[:, layer, seg, :], src, bias, ALU.add).then_inc(mod_step, 1)
                made[0] += 1
                dve.wait_ge(mod_step, made[0])
                gate = seg in (GATE_M, GATE_F)
                g = V_NORM_G + (layer * 4 + 2 * mlp + gate) * NC
                nc.vector.scalar_tensor_tensor(out=mod[:, layer, 3 * mlp + 2 * gate, :], in0=mod_t[:, layer, seg, :],
                                               scalar=0.0 if gate else 1.0, in1=vec[:, g:g + NC], op0=ALU.add,
                                               op1=ALU.mult).then_inc(mod_ready, 1)

            made = [0]

            def later_mods(b, which):
                done = {1: (5, 6), 2: (8, 9), 3: (11, 12)}[b][which]
                for i, s in enumerate(LATER[b][which]):
                    make_mod(done + len(LATER[b][which]), min(s, 1), GATE_F if s == 0 else s - 1, which, 8 * i)

            def reciprocal_rms(k):
                dve.wait_ge(std_done, k + 1)
                nc.vector.reciprocal(std[:, 1, :], std[:, 0, :]).then_inc(rs_done, 1)
                dve.wait_ge(rs_done, k + 1)
                for j in range(NT):
                    op = nc.vector.tensor_scalar(diag[:, j, :], ident[:, :], std[:, 1, j:j + 1], None, ALU.mult)
                op.then_inc(diag_done, 1)

            def add_square(b, n):
                dve.wait_ge(y_sq, NC * b + n + 1)
                if n >= 2:
                    dve.wait_ge(ssq_step, (NC - 1) * b + n - 1)
                nc.vector.tensor_tensor(ssq[:, :], ssq[:, :], sq[:, n % 2, 0:T], ALU.add).then_inc(ssq_step, 1)

            def boundary(b):
                if b in LATER:
                    later_mods(b, 0)
                reciprocal_rms(2 * b + 1)
                dve.wait_ge(mod_ready, GATE_MODS[b])
                dve.wait_ge(bcast_done, 2 * b + 2)
                layer, g = GATES[b]
                for n in range(NC + 1):
                    if n < NC:
                        nc.vector.tensor_tensor(y[:, n, :], y[:, n, :], ps[:, BCAST_BANK, :], ALU.mult).then_inc(y_norm, 1)
                    if n >= 1:
                        dve.wait_ge(y_norm, NC * b + n)
                        nc.vector.scalar_tensor_tensor(out=xs[:, n - 1, :], in0=y[:, n - 1, :], scalar=mod[:, layer, g, n - 1:n],
                                                       in1=xs[:, n - 1, :], op0=ALU.mult, op1=ALU.add).then_inc(x_new, 1)
                if b == 3:
                    for j in (2, 3):
                        dve.wait_ge(out_turned, NC)
                        nc.vector.tensor_copy(x_tok[:, j, T:2 * T], ps[:, j, :]).then_inc(out_by_dve, 1)
                    return
                if b in LATER:
                    later_mods(b, 1)
                reciprocal_rms(2 * b + 2)
                dve.wait_ge(mod_ready, INPUT_MODS[b])
                dve.wait_ge(bcast_done, 2 * b + 3)
                layer, a = INPUTS[b]
                for n in range(NC + 2):
                    if n < NC:
                        dve.wait_ge(x_new, NC * b + n + 1)
                        nc.vector.tensor_tensor(y[:, n, :], xs[:, n, :], ps[:, BCAST_BANK, :], ALU.mult).then_inc(h_norm, 1)
                    if 1 <= n <= NC:
                        m = n - 1
                        dve.wait_ge(h_norm, NC * b + m + 1)
                        nc.vector.tensor_scalar(y[:, m, :], y[:, m, :], mod[:, layer, a, m:m + 1], mod[:, layer, a + 1, m:m + 1],
                                                ALU.mult, ALU.add).then_inc(h_full, 1)
                    if n >= 2:
                        m = n - 2
                        dve.wait_ge(h_hi, NC * (b + 1) + m + 1)
                        nc.vector.tensor_tensor(in_lo[:, m, :], y[:, m, :], in_hi[:, m, :].bitcast(F32), ALU.subtract).then_inc(h_lo, 1)

            def mlp_quarter(layer, q, last=False):
                b = 1 + 2 * layer
                for j in range(Q_UNITS):
                    u = FFN_U[layer] + j
                    if j in (1, 3):
                        for m in range(BANKS):
                            n = BANKS * (j // 2) + m
                            i = layer * QUARTERS * NC + n
                            dve.wait_ge(hid_hi, q * NC + (i + 1))
                            nc.vector.tensor_tensor(relu[:, n % 2, 0:T], relu[:, n % 2, 0:T], relu[:, n % 2, 0:T], ALU.mult).then_inc(hid_sq, 1)
                            dve.wait_ge(hid_sq, q * NC + (i + 1))
                            nc.vector.tensor_tensor(mid_lo[:, n, :], relu[:, n % 2, 0:T], mid_hi[:, n, :].bitcast(F32), ALU.subtract).then_inc(hid_lo, 1)
                    if j in (5, 7):
                        dve.wait_ge(y_zero, layer + 1)
                        for m in range(BANKS):
                            n = BANKS * (j // 2 - 2) + m
                            group = NC + BANKS * pair(u) + m + 1
                            dve.wait_ge(bank_done, q * (BANKS * Q_UNITS // 2) + group)
                            nc.vector.tensor_tensor(y[:, n, :], y[:, n, :], ps[:, BANKS * (j // 2 - 2) + m, :], ALU.add).then_inc(y_sum, 1)
                            if last and n >= 2:
                                add_square(b, n - 1)
                        if last and j == 7:
                            add_square(b, NC - 1)
                    if layer == 0 and j < LATER_SEGS:
                        dve.wait_ge(sums_zero, 1)
                        for i in (2 * j, 2 * j + 1):
                            dve.wait_ge(ada_used, q * ADA_Q + (ADA_FIRST + i - LATER_SEGS + 1))
                            landed = q * (16 * LATER_SEGS) + 16 * (ADA_FIRST // ADA_SLOTS + i // 2 + 1)
                            k = q * 2 + i // LATER_SEGS
                            c_col = silu_t[:, 3, k:k + 1] if isinstance(q, int) else silu_t[:, 3, bass.ds(k, 1)]
                            add_ada(None, i % 2, landed, i % LATER_SEGS, c_col, False)
                    if not (last and u + Q_UNITS * q + 2 >= UNITS):
                        split_lo(u + 2, q)

            dve.wait_ge(exp_ready, 1)
            nc.vector.tensor_scalar(silu_t[:, 1, :], silu_t[:, 0, :], 1.0, None, ALU.add).then_inc(silu_step, 1)
            dve.wait_ge(silu_step, 1)
            nc.vector.reciprocal(silu_t[:, 2, :], silu_t[:, 1, :]).then_inc(silu_step, 1)
            dve.wait_ge(silu_step, 2)
            nc.vector.tensor_tensor(silu_t[:, 3, :], silu_t[:, 2, :], vec[:, V_C:V_END], ALU.mult).then_inc(silu_step, 1)
            dve.wait_ge(silu_step, 3)

            for a in range(4):
                first_ada(a)
            reciprocal_rms(0)
            for a in range(4, 2 * NC):
                if a % 4 == 0:
                    g = a // 4 - 1
                    dve.wait_ge(bcast_done, 1)
                    dve.wait_ge(x_copied, 2 * g + 2)
                    if g >= 2:
                        dve.wait_ge(window_ready, g - 1)
                    for n in (2 * g, 2 * g + 1):
                        nc.vector.tensor_tensor(norm0[:, n % 4, :], xs[:, n, :], ps[:, BCAST_BANK, :], ALU.mult).then_inc(norm0_ready, 1)
                first_ada(a)
            dve.wait_ge(window_ready, 2)
            for n in (6, 7):
                nc.vector.tensor_tensor(norm0[:, n % 4, :], xs[:, n, :], ps[:, BCAST_BANK, :], ALU.mult).then_inc(norm0_ready, 1)
            for i, seg in enumerate(FIRST_SEGS[:2]):
                make_mod(i + 1, 0, seg, 4 + i, 0)
            split_lo(POOL_U)
            for n in range(NC + 2):
                first_ada(2 * NC + 2 * n)
                first_ada(2 * NC + 2 * n + 1)
                if n < NC:
                    dve.wait_ge(window_ready, min(n // 2 + 3, 4))
                    if n >= 4:
                        dve.wait_ge(pool_diff, n - 3)
                    nc.vector.tensor_tensor(norm0[:, n % 4, :], xs[:, n, :], ps[:, BCAST_BANK, :], ALU.mult).then_inc(pool_t, 1)
                if 1 <= n <= NC:
                    dve.wait_ge(pool_h, n)
                    nc.vector.tensor_tensor(y[:, n - 1, :], y[:, n - 1, :], norm0[:, (n - 1) % 4, :], ALU.subtract).then_inc(pool_diff, 1)
                if n >= 2:
                    dve.wait_ge(h_hi, n - 1)
                    nc.vector.tensor_tensor(in_lo[:, n - 2, :], y[:, n - 2, :], in_hi[:, n - 2, :].bitcast(F32), ALU.subtract).then_inc(h_lo, 1)
            for a in range(2 * NC + 2 * (NC + 2), ADA_FIRST):
                first_ada(a)
            for n in range(1, NC):
                add_square(0, n)
            split_lo(1)
            for i, seg in enumerate(FIRST_SEGS[2:]):
                make_mod(len(FIRST_SEGS), 0, seg, 5, 8 * i)
            split_lo(2)
            boundary(0)
            with dve.Fori(0, QUARTERS - 1) as q:
                mlp_quarter(0, q)
            mlp_quarter(0, QUARTERS - 1, last=True)
            boundary(1)
            dve.wait_ge(cu_pad, 1)
            for g in range(6):
                u = CONV_U + 2 * g
                split_lo(u + 2)
                if g in CV_GROUPS:
                    for p in (0, 1):
                        n = 2 * CV_GROUPS.index(g) + p
                        dve.wait_ge(bank_done, NC + BANKS * pair(u) + 2 * p + 2)
                        dve.wait_ge(c_copied, n + 1)
                        nc.vector.tensor_tensor(cu[:, p, 1:T + 1], cgate[:, p, :], ps[:, BANKS * (g % 2) + 2 * p + 1, :], ALU.mult).then_inc(cu_ready, 1)
                        dve.wait_ge(z_mid, n + 1)
                        nc.vector.scalar_tensor_tensor(out=y[:, n, :], in0=cu[:, p, 0:T], scalar=col(V_CONV, n), in1=y[:, n, :],
                                                       op0=ALU.mult, op1=ALU.add).then_inc(z_left, 1)
                        dve.wait_ge(z_left, n + 1)
                        nc.vector.scalar_tensor_tensor(out=y[:, n, :], in0=cu[:, p, 2:T + 2], scalar=col(V_CONV + 2 * NC, n), in1=y[:, n, :],
                                                       op0=ALU.mult, op1=ALU.add).then_inc(z_ready, 1)
                else:
                    for m in range(BANKS):
                        n = BANKS * (g // 3) + m
                        dve.wait_ge(bank_done, NC + BANKS * pair(u) + m + 1)
                        dve.wait_ge(z_ready, n + 1)
                        nc.vector.tensor_tensor(y[:, n, :], y[:, n, :], ps[:, BANKS * (g % 2) + m, :], ALU.mult).then_inc(gated, 1)
                        dve.wait_ge(g_hi, n + 1)
                        nc.vector.tensor_tensor(mid_lo[:, n, :], y[:, n, :], mid_hi[:, n, :].bitcast(F32), ALU.subtract).then_inc(g_lo, 1)
                split_lo(u + 3)
            for g in range(2):
                u = OUT_U + 2 * g
                split_lo(u + 2)
                for m in range(BANKS):
                    if BANKS * g + m:
                        add_square(2, BANKS * g + m)
                split_lo(u + 3)
            boundary(2)
            with dve.Fori(0, QUARTERS - 1) as q:
                mlp_quarter(1, q)
            mlp_quarter(1, QUARTERS - 1, last=True)
            boundary(3)

        @block.gpsimd
        def _(pool):
            nc.gpsimd.memset(ident[:, :], 0.0).then_inc(ident_zero, 1)
            nc.gpsimd.memset(ones[:, :], 1.0).then_inc(consts_ready, 1)
            pool.wait_ge(ident_zero, 1)
            nc.gpsimd.affine_select(out=ident[:, :], in_=ident[:, :], compare_op=ALU.not_equal, fill=1.0, base=0,
                                    pattern=[[-1, P]], channel_multiplier=1).then_inc(consts_ready, 1)
            nc.gpsimd.memset(eps[:, :], EPS).then_inc(eps_ready, 1)
            steps = [0]

            def step(op):
                steps[0] += 1
                op.then_inc(level_step, 1)
                pool.wait_ge(level_step, steps[0])

            at = 0
            for w in WINDOWS:
                half = w // 2
                for n in [t + half for t in range(half)] + [w - 1 - r for r in range(half - 1)]:
                    op = nc.gpsimd.memset(edge[:, :, at:at + 1], w / n)
                    at += 1
            step(op)
            pool.wait_ge(x_stat, NC)
            at = 0
            for g, w in enumerate(WINDOWS):
                half = w // 2
                t0 = norm0[:, 2 * (g % 2):2 * (g % 2) + 2, :]
                nc.gpsimd.memset(relu[:, :, 0:PAD], 0.0)
                step(nc.gpsimd.memset(relu[:, :, PAD + T:LEVEL], 0.0))
                pool.wait_ge(norm0_ready, 2 * g + 2)
                nc.gpsimd.tensor_copy(relu[:, :, PAD - 1:PAD], t0[:, :, 0:1])
                nc.gpsimd.tensor_copy(relu[:, :, PAD + T - 1:PAD + T], t0[:, :, T - 1:T])
                step(nc.gpsimd.tensor_tensor(relu[:, :, PAD:PAD + T - 1], t0[:, :, 0:T - 1], t0[:, :, 1:T], ALU.add))
                src, other, width, end = relu, sq, 2, LEVEL - 2
                while width < w:
                    end -= width
                    step(nc.gpsimd.tensor_tensor(other[:, :, 0:end], src[:, :, 0:end], src[:, :, width:width + end], ALU.add))
                    src, other, width = other, src, 2 * width
                lo = PAD - half
                nc.gpsimd.tensor_tensor(src[:, :, lo:lo + half], src[:, :, lo:lo + half], edge[:, :, at:at + half], ALU.mult)
                if half > 1:
                    r = slice(lo + T - half + 1, lo + T)
                    nc.gpsimd.tensor_tensor(src[:, :, r], src[:, :, r], edge[:, :, at + half:at + w - 1], ALU.mult)
                step(nc.gpsimd.memset(edge[:, :, 31:32], 0.0))
                at += w - 1
                nc.gpsimd.tensor_scalar(y[:, 2 * g:2 * g + 2, :], src[:, :, lo:lo + T], 1.0 / w, None, ALU.mult).then_inc(window_ready, 1)
                pool.wait_ge(window_ready, g + 1)
            pool.wait_ge(ada_cols, len(FIRST_SEGS))
            pool.wait_ge(pool_diff, NC)
            nc.gpsimd.memset(ada_sum[:, :, :], 0.0).then_inc(sums_zero, 1)
            pool.wait_ge(h_lo, 2 * NC)
            nc.gpsimd.memset(y[:, :, :], 0.0).then_inc(y_zero, 1)
            pool.wait_ge(ada_cols, len(FIRST_SEGS) + 3)
            nc.gpsimd.memset(cu[:, :, 0:1], 0.0)
            nc.gpsimd.memset(cu[:, :, T + 1:T + 2], 0.0).then_inc(cu_pad, 1)
            pool.wait_ge(h_lo, 4 * NC)
            nc.gpsimd.memset(y[:, :, :], 0.0).then_inc(y_zero, 1)


_INS = ['x', 'c', 'ada_w', 'ada_b', 'norm_g', 'ffn_w1', 'ffn_w2', 'pool_w', 'pool_scale', 'conv_in_w', 'conv_w', 'conv_out_w']


def kernel(**inputs):
    import numpy as _np
    import concourse.bacc as _bacc
    from concourse import mybir as _mybir
    from concourse.bass_utils import run_bass_kernel_spmd as _run

    nc = _bacc.Bacc("TRN2", target_bir_lowering=False, num_devices=1)
    arrays, args = {}, []
    for name in _INS:
        a = _np.ascontiguousarray(inputs[name])
        arrays[f"in_{name}_dram"] = a
        args.append(nc.dram_tensor(f"in_{name}_dram", a.shape, _mybir.dt.from_np(a.dtype), kind="ExternalInput").ap())
    args.append(nc.dram_tensor("out_dram", (1, T, D), _mybir.dt.float32, kind="ExternalOutput").ap())
    trunk(nc, *args)
    r = _run(nc, [arrays], core_ids=[0])
    return r.results[0]["out_dram"]
```

```python
from contextlib import ExitStack

import concourse.bass as bass
from concourse import mybir

F32 = mybir.dt.float32
F32R = mybir.dt.float32r
ALU = mybir.AluOpType
ACT = mybir.ActivationFunctionType

P = 128
D = 1024
NC = D // P
T = 512
NT = T // P
FF = 4096
EPS = 1e-6
WINDOWS = (2, 4, 8, 16)
GROUP = D // len(WINDOWS)
PAD = max(WINDOWS) // 2
LEVEL = T + 2 * PAD

UK, UN = 4, 512
BANKS = UN // P
QUARTERS = 4
QF = FF // QUARTERS
Q_UNITS = 8
POOL_U = 0
FFN_U = (1, 1 + 4 * Q_UNITS + 16)
CONV_U = 1 + 4 * Q_UNITS
OUT_U = CONV_U + 12
UNITS = FFN_U[1] + 4 * Q_UNITS
RAW_SLOTS = 2
CV_GROUPS = (0, 1, 3, 4)
CV_COLS = (0, 256, 128, 384)

SHIFT_M, SCALE_M, GATE_M, SHIFT_F, SCALE_F, GATE_F = range(6)
FIRST_SEGS = (SCALE_M, SHIFT_M, GATE_M, SCALE_F, SHIFT_F)
LATER_SEGS = 7
ADA_SLOTS = 3
ADA_FIRST = len(FIRST_SEGS) * NC
ADA_Q = 2 * LATER_SEGS
LOOP_Q = QUARTERS - 1
LAST_STEPS = (3, 3, 3, 3, 2, 0, 0, 0)

V_ADA_B = 0
V_NORM_G = 2 * 6 * NC
V_POOL = V_NORM_G + 2 * 4 * NC
V_CONV = V_POOL + NC
V_C = V_CONV + 3 * NC
V_END = V_C + NC

POOL_ORDER = (6, 7, 4, 5, 2, 3, 0, 1)
POOL_BANK = (0, 1, 2, 3, 4, 6, 7, 0)
R_BANK, R2_BANK, Y_BANK, XV_BANK = 6, 5, 7, 4


def trunk(nc, x, c, ada_w, ada_b, norm_g, ffn_w1, ffn_w2, pool_w, pool_scale, conv_in_w, conv_w, conv_out_w, out):
    with ExitStack() as ctx:
        def sb(name, shape, dt=F32):
            return ctx.enter_context(nc.sbuf_tensor(name, shape, dt))

        def sem(name):
            return ctx.enter_context(nc.semaphore(name))

        xs = sb("xs", [P, NC, T])
        in_hi = sb("in_hi", [P, NC, T], F32R)
        in_lo = sb("in_lo", [P, NC, T], F32R)
        mid_hi = sb("mid_hi", [P, NC, T], F32R)
        mid_lo = sb("mid_lo", [P, NC, T], F32R)
        y = sb("y", [P, NC, T])
        raw = sb("raw", [P, RAW_SLOTS, UK * UN])
        w_hi = sb("w_hi", [P, 2, UK * UN], F32R)
        w_lo = sb("w_lo", [P, 2, UK * UN], F32R)
        ada_raw = sb("ada_raw", [P, ADA_SLOTS, D])
        ada_sum = sb("ada_sum", [P, LATER_SEGS, D])
        work = sb("work", [P, 2, 3, T])
        sums = sb("sums", [P, 3, T])
        vec = sb("vec", [P, V_END])
        mod = sb("mod", [P, 2, 6, NC])
        mod_t = sb("mod_t", [P, 2, 6, NC])
        silu_t = sb("silu_t", [P, 4, NC])
        rms_y = sb("rms_y", [P, 2, NT])
        rms_x = sb("rms_x", [P, 2, NT])
        xx = sb("xx", [P, NT])
        xx_t = sb("xx_t", [P, 5, NT])
        edge = sb("edge", [P, 2, 32])
        ident = sb("ident", [P, P])
        ones = sb("ones", [P, P])
        eps = sb("eps", [P, 1])
        note = sb("note", [P, 2])
        a_by_w = sb("a_by_w", [P, NC])
        ps = ctx.enter_context(nc.psum_tensor("ps", [P, 8, T], F32))

        x_tok = raw[:, :, :].rearrange("p s (j d) -> p (s j) d", d=D)
        relu = work[:, :, 0, :]
        vec_rows = work[:, 0, 0, 0:2 * P].rearrange("p (s n) -> p s n", s=2)
        level = [work[:, s, :, :].rearrange("p a t -> p (a t)")[:, 0:2 * LEVEL].rearrange("p (a t) -> p a t", a=2) for s in range(2)]
        diag_y = work[:, 0, 0, :].rearrange("p (j q) -> p j q", j=NT)
        diag_x = work[:, 0, 1, :].rearrange("p (j q) -> p j q", j=NT)
        norm_lo = ada_sum[:, 5:7, :].rearrange("p s (a t) -> p (s a) t", a=2)
        norm_hi = raw[:, 1, :].rearrange("p (a t) -> p a t", a=4)

        def norm0(n, k=1):
            return norm_lo[:, n:n + k, :] if n < 4 else norm_hi[:, n - 4:n - 4 + k, :]

        flat = ada_sum[:, :, :].rearrange("p s d -> p (s d)")
        cgate = flat[:, 0:2 * T].rearrange("p (s t) -> p s t", s=2)
        cu = flat[:, 2 * T:2 * T + 2 * (T + 2)].rearrange("p (s t) -> p s t", s=2)


        x_in, vec_in, out_done = sem("x_in"), sem("vec_in"), sem("out_done")
        raw_in = [sem(f"raw_in{s}") for s in range(RAW_SLOTS)]
        ada_in = [sem(f"ada_in{s}") for s in range(ADA_SLOTS)]
        consts_ready, ident_zero, eps_ready = sem("consts_ready"), sem("ident_zero"), sem("eps_ready")
        vec_turned, vec_ready = sem("vec_turned"), sem("vec_ready")
        exp_ready, silu_step = sem("exp_ready"), sem("silu_step")
        x_turned, x_copied = sem("x_turned"), sem("x_copied")
        w_hi_ready, w_lo_ready, w_lo_by_pool = sem("w_hi_ready"), sem("w_lo_ready"), sem("w_lo_by_pool")
        unit_done, bank_done = sem("unit_done"), sem("bank_done")
        ada_used, ada_cols, mod_step, mod_ready, sums_zero = sem("ada_used"), sem("ada_cols"), sem("mod_step"), sem("mod_ready"), sem("sums_zero")
        norm0_ready, level_step, window_ready = sem("norm0_ready"), sem("level_step"), sem("window_ready")
        mean_scale = sem("mean_scale")
        pool_mean, pool_h, pool_diff = sem("pool_mean"), sem("pool_h"), sem("pool_diff")
        relu_done, hid_hi, hid_sq, hid_lo = sem("relu_done"), sem("hid_hi"), sem("hid_sq"), sem("hid_lo")
        y_zero, y_sum, y_copied = sem("y_zero"), sem("y_sum"), sem("y_copied")
        y_sq, v_ready, v_sq = sem("y_sq"), sem("v_ready"), sem("v_sq")
        yy_added, xv_ready, xv_added, x_sq = sem("yy_added"), sem("xv_ready"), sem("xv_added"), sem("x_sq")
        yy_cols, xv_cols, xx_step, xx_ready = sem("yy_cols"), sem("xv_cols"), sem("xx_step"), sem("xx_ready")
        rms_ready, rcp_ready, diag_ready, bcast_done = sem("rms_ready"), sem("rcp_ready"), sem("diag_ready"), sem("bcast_done")
        y_norm, x_new = sem("y_norm"), sem("x_new")
        h_norm, h_full, h_hi, h_lo = sem("h_norm"), sem("h_full"), sem("h_hi"), sem("h_lo")
        c_copied, cu_ready, cu_pad = sem("c_copied"), sem("cu_ready"), sem("cu_pad")
        z_mid, z_left, z_ready = sem("z_mid"), sem("z_left"), sem("z_ready")
        gated, g_hi, g_lo = sem("gated"), sem("g_hi"), sem("g_lo")
        out_turned, out_by_act, out_by_dve = sem("out_turned"), sem("out_by_act"), sem("out_by_dve")

        block = ctx.enter_context(nc.Block())

        def pair(u):
            return (u - 1) // 2

        def unit_wait(eng, first, pairs):
            if first:
                eng.wait_ge(unit_done, pairs + 1)
            else:
                eng.wait_ge(bank_done, NC + BANKS * (pairs + 1))

        def raw_value(u):
            n = 0
            for v in range(u % 2, u + 1, 2):
                n += 32 if CONV_U <= v < OUT_U and (v - CONV_U) // 2 in CV_GROUPS else 16
            return n

        def col(base, chunk):
            return vec[:, base + chunk:base + chunk + 1]

        GATES = ((0, 2), (0, 5), (1, 2), (1, 5))
        INPUTS = ((0, 3), (1, 0), (1, 3))
        VECTORS = ((0, 0, SCALE_M, 4), (1, 0, SHIFT_M, 5),
                   (2, 0, GATE_M, 5),
                   (3, 0, SCALE_F, 1), (4, 0, SHIFT_F, 2),
                   (0, 0, GATE_F, 0),
                   (1, 1, SHIFT_M, 1), (2, 1, SCALE_M, 2), (3, 1, GATE_M, 3),
                   (4, 1, SHIFT_F, 1), (5, 1, SCALE_F, 2), (6, 1, GATE_F, 3))
        AT_BOUNDARY = ((3, 4, None), (6, 7, 8), (9, 10, 11), (None, None, None))
        GATE_MADE = (3, 6, 9, 12)
        INPUT_MADE = (5, 8, 11)
        SECOND = (FFN_U[0] + 1, CONV_U + 1, FFN_U[1] + 1)

        def add_wait(eng, sem_x, value):
            if isinstance(value, int) and value <= 0:
                return
            eng.wait_ge(sem_x, value)

        def split_wait(eng, u, q=0):
            eng.wait_ge(w_lo_ready, q * Q_UNITS + (u + 1))

        def ada_landed(i, last):
            n = [len(range(s, ADA_FIRST, ADA_SLOTS)) for s in range(ADA_SLOTS)]
            if last:
                return 16 * (n[i % 3] + (LOOP_Q * LATER_SEGS if i % 3 < 2 else 0) + i // 3 + 1)
            return 16 * (n[i % 2] + i // 2 + 1)

        def last_units(j):
            at = sum(LAST_STEPS[:j])
            return range(at, at + LAST_STEPS[j])

        def raw_cols(slot, cols=slice(0, UN)):
            return raw[:, slot, :].rearrange("p (k n) -> p k n", k=UK)[:, :, cols]

        def w_rows(w):
            return w.rearrange("(k p) n -> p k n", p=P)

        @block.sync
        def _(sp):
            sp.dma_start(vec_rows[0:V_NORM_G, 0, :], ada_b.rearrange("l (r p) -> (l r) p", p=P)).then_inc(vec_in, 16)
            at = 0
            for v, n in ((norm_g.rearrange("l g (r p) -> (l g r) p", p=P), V_POOL - V_NORM_G),
                         (pool_scale.rearrange("l (r p) -> (l r) p", p=P), NC),
                         (conv_w.rearrange("l w (r p) -> (l w r) p", p=P), 3 * NC),
                         (c.rearrange("l (r p) -> (l r) p", p=P), NC)):
                sp.dma_start(vec_rows[at:at + n, 1, :], v).then_inc(vec_in, 16)
                at += n
            for j in range(NT):
                sp.dma_start(x_tok[:, j, :], x[0, j * P:(j + 1) * P, :]).then_inc(x_in, 16)

            def load_ada(a):
                if a >= ADA_SLOTS:
                    sp.wait_ge(ada_used, a - ADA_SLOTS + 1)
                seg, k = FIRST_SEGS[a // NC], a % NC
                sp.dma_start(ada_raw[:, a % ADA_SLOTS, :],
                             ada_w[0, k * P:(k + 1) * P, seg * D:(seg + 1) * D]).then_inc(ada_in[a % ADA_SLOTS], 16)

            def load_mlp(layer):
                with sp.Fori(0, QUARTERS) as q:
                    for j in range(Q_UNITS):
                        u = FFN_U[layer] + j
                        split_wait(sp, max(u - 2, 0), q)
                        if j < 4:
                            src = ffn_w1[layer, (j % 2) * UK * P:(j % 2 + 1) * UK * P,
                                         bass.ds(q * QF + (j // 2) * UN, UN)]
                        else:
                            src = ffn_w2[layer, bass.ds(q * QF + (j % 2) * UK * P, UK * P),
                                         (j // 2 - 2) * UN:(j // 2 - 1) * UN]
                        sp.dma_start(raw_cols(u % 2), w_rows(src)).then_inc(raw_in[u % 2], 16)

            for a in range(2 * NC):
                load_ada(a)
            sp.wait_ge(x_turned, NC)
            sp.dma_start(raw[:, 0, :].rearrange("p (g n) -> p g n", g=2 * len(WINDOWS)),
                         pool_w[0].rearrange("g (k p) n -> p (g k) n", p=P)).then_inc(raw_in[0], 16)
            for a in range(2 * NC, ADA_FIRST):
                load_ada(a)
            sp.wait_ge(pool_diff, NC)
            load_mlp(0)
            for u in range(CONV_U, FFN_U[1]):
                split_wait(sp, u - 2)
                if u < OUT_U:
                    g, kk = (u - CONV_U) // 2, (u - CONV_U) % 2
                    rows = conv_in_w[0, kk * UK * P:(kk + 1) * UK * P, :]
                    if g in CV_GROUPS:
                        n = CV_GROUPS.index(g) * UN // 2
                        for i in (0, 1):
                            sp.dma_start(raw_cols(u % 2, slice(i * UN // 2, (i + 1) * UN // 2)),
                                         w_rows(rows[:, (1 + i) * D + n:(1 + i) * D + n + UN // 2])).then_inc(raw_in[u % 2], 16)
                    else:
                        n = (g // 3) * UN
                        sp.dma_start(raw_cols(u % 2), w_rows(rows[:, n:n + UN])).then_inc(raw_in[u % 2], 16)
                else:
                    g, kk = (u - OUT_U) // 2, (u - OUT_U) % 2
                    sp.dma_start(raw_cols(u % 2), w_rows(conv_out_w[0, kk * UK * P:(kk + 1) * UK * P,
                                                                    g * UN:(g + 1) * UN])).then_inc(raw_in[u % 2], 16)
            load_mlp(1)
            for half in range(2):
                for j in range(NT):
                    if half == 1 and j >= 2:
                        sp.wait_ge(out_by_dve, j - 1)
                    else:
                        sp.wait_ge(out_by_act, half * NT + j + 1)
                    sp.dma_start(out[0, j * P:(j + 1) * P, half * T:(half + 1) * T],
                                 x_tok[:, j, half * T:(half + 1) * T]).then_inc(out_done, 16)
            sp.wait_ge(out_done, 16 * 2 * NT)

        @block.tensor
        def _(pe):
            def multiply(u, q, hi, lo, chunks, need, rows_first=False, cols=None):
                first = (u - 1) % 2 == 0
                banks = [BANKS * (pair(u) % 2) + m for m in range(BANKS)]
                cols = cols or [m * P for m in range(BANKS)]
                split_wait(pe, u, q)

                def products(kk, m):
                    n = kk * UN + cols[m]
                    a, b = w_hi[:, u % 2, n:n + P], w_lo[:, u % 2, n:n + P]
                    o = ps[:, banks[m], :]
                    nc.tensor.matmul(o, a, hi[:, chunks[kk], :], start=first and kk == 0, stop=False)
                    nc.tensor.matmul(o, a, lo[:, chunks[kk], :], start=False, stop=False)
                    return nc.tensor.matmul(o, b, hi[:, chunks[kk], :], start=False, stop=not first and kk == UK - 1)

                if first or rows_first:
                    for kk in range(UK):
                        need(kk)
                        for m in range(BANKS):
                            last = products(kk, m)
                            if not first and kk == UK - 1:
                                last.then_inc(bank_done, 1)
                    if first:
                        last.then_inc(unit_done, 1)
                else:
                    need(UK - 1)
                    for m in range(BANKS):
                        for kk in range(UK):
                            last = products(kk, m)
                        last.then_inc(bank_done, 1)

            def mlp_unit(layer, q, j):
                u = FFN_U[layer] + j
                half = UK * (j % 2)
                chunks = [half + kk for kk in range(UK)]
                if j < 4:
                    multiply(u, q, in_hi, in_lo, chunks,
                             lambda kk, n=NC * (1 + 2 * layer) + half: pe.wait_ge(h_lo, n + kk + 1), rows_first=j == 1)
                else:
                    multiply(u, q, mid_hi, mid_lo, chunks,
                             lambda kk, n=layer * QUARTERS * NC + half: pe.wait_ge(hid_lo, q * NC + (n + kk + 1)))

            def stat_cols(bank, at, src):
                for j in range(NT):
                    mm = nc.tensor.matmul(ps[:, bank, at + j:at + j + 1], src[:, j * P:(j + 1) * P], ones[:, 0:1],
                                          start=True, stop=True)
                return mm

            def broadcast(k):
                pe.wait_ge(diag_ready, k + 1)
                nc.tensor.matmul(ps[:, R_BANK if k % 2 or k == 0 else R2_BANK, :], ones[:, :], diag_y if k % 2 else diag_x,
                                 start=True, stop=True).then_inc(bcast_done, 1)

            def reduce_vector(i):
                if i is None:
                    return
                s, _, _, bank = VECTORS[i]
                pe.wait_ge(ada_used, NC * (i + 1) if i < 5 else ADA_FIRST + QUARTERS * ADA_Q)
                for m in range(NC):
                    mm = nc.tensor.matmul(ps[:, bank, m:m + 1], ada_sum[:, s, m * P:(m + 1) * P], ones[:, 0:1],
                                          start=True, stop=True)
                mm.then_inc(ada_cols, 1)

            def boundary(b):
                first, second, third = AT_BOUNDARY[b]
                if first is not None:
                    pe.wait_ge(y_sq, NC * b + 4)
                    pe.wait_ge(v_ready, NC * b + 4)
                reduce_vector(first)
                pe.wait_ge(v_ready, NC * (b + 1))
                pe.wait_ge(yy_added, (NC - 1) * (b + 1) + NC - 1)
                stat_cols(Y_BANK, 0, sums[:, 0, :]).then_inc(yy_cols, 1)
                reduce_vector(second)
                if b == 3:
                    broadcast(7)
                    for n in range(NC):
                        pe.wait_ge(x_new, NC * 3 + n + 1)
                        if n == 4:
                            pe.wait_ge(out_by_act, NT)
                        for j in range(NT):
                            tr = nc.tensor.transpose(ps[:, j, (n % 4) * P:(n % 4 + 1) * P], xs[:, n, j * P:(j + 1) * P], ident[:, :])
                        tr.then_inc(out_turned, 1)
                    return
                pe.wait_ge(xv_added, (NC - 1) * (b + 1))
                stat_cols(XV_BANK, 0, sums[:, 1, :])
                stat_cols(XV_BANK, NT, sums[:, 2, :]).then_inc(xv_cols, 1)
                broadcast(2 * b + 1)
                reduce_vector(third)
                broadcast(2 * b + 2)

            pe.wait_ge(consts_ready, 2)
            pe.wait_ge(vec_in, 16 * 5)
            for s, (n, at) in enumerate(((V_NORM_G, 0), (V_END - V_NORM_G, V_NORM_G))):
                tr = nc.tensor.transpose(ps[:, 5, at:at + n], vec_rows[0:n, s, :], ident[0:n, 0:n])
            tr.then_inc(vec_turned, 1)
            pe.wait_ge(x_in, 16 * NT)
            for n in range(NC):
                if n >= 4:
                    pe.wait_ge(x_sq, n - 3)
                for j in range(NT):
                    tr = nc.tensor.transpose(ps[:, n % 4, j * P:(j + 1) * P], x_tok[:, j, n * P:(n + 1) * P], ident[:, :])
                tr.then_inc(x_turned, 1)
            pe.wait_ge(yy_added, NC - 1)
            stat_cols(Y_BANK, 0, sums[:, 0, :]).then_inc(yy_cols, 1)
            broadcast(0)
            reduce_vector(0)
            reduce_vector(1)
            pe.wait_ge(w_lo_ready, 1)
            for i, n in enumerate(POOL_ORDER):
                if i == 4:
                    reduce_vector(2)
                if i == 7:
                    pe.wait_ge(y_copied, 1)
                g, bank = n // 2, ps[:, POOL_BANK[i], :]
                for kk in range(2):
                    pe.wait_ge(h_lo, 2 * (i // 2) + kk + 1)
                    at = (2 * g + kk) * GROUP + (n % 2) * P
                    a, b = w_hi[:, 0, at:at + P], w_lo[:, 0, at:at + P]
                    nc.tensor.matmul(bank, a, in_hi[:, 2 * g + kk, :], start=kk == 0, stop=False)
                    nc.tensor.matmul(bank, a, in_lo[:, 2 * g + kk, :], start=False, stop=False)
                    mm = nc.tensor.matmul(bank, b, in_hi[:, 2 * g + kk, :], start=False, stop=kk == 1)
                mm.then_inc(bank_done, 1)
            boundary(0)
            with pe.Fori(0, LOOP_Q) as q:
                for j in range(Q_UNITS):
                    mlp_unit(0, q, j)
            for j in range(Q_UNITS):
                if j == 6:
                    pe.wait_ge(y_sum, NC * LOOP_Q + 1)
                    reduce_vector(5)
                mlp_unit(0, LOOP_Q, j)
            boundary(1)
            for g in range(6):
                for kk in (0, 1):
                    multiply(CONV_U + 2 * g + kk, 0, in_hi, in_lo, [UK * kk + i for i in range(UK)],
                             lambda i, n=NC * 2 + UK * kk: pe.wait_ge(h_lo, n + i + 1), rows_first=g == 0,
                             cols=CV_COLS if g in CV_GROUPS else None)
            for g in range(2):
                for kk in (0, 1):
                    multiply(OUT_U + 2 * g + kk, 0, mid_hi, mid_lo, [UK * kk + i for i in range(UK)],
                             lambda i, n=UK * kk: pe.wait_ge(g_lo, n + i + 1))
            boundary(2)
            with pe.Fori(0, QUARTERS) as q:
                for j in range(Q_UNITS):
                    mlp_unit(1, q, j)
            boundary(3)

        @block.scalar
        def _(act):
            def split_hi(u, q=0):
                raw_at = raw_value(u + Q_UNITS * q) if isinstance(q, int) else q * (16 * Q_UNITS // 2) + raw_value(u)
                act.wait_ge(raw_in[u % 2], raw_at)
                if u == 2:
                    act.wait_ge(bank_done, NC)
                elif u > 2:
                    unit_wait(act, (u - 3) % 2 == 0, q * (Q_UNITS // 2) + pair(u - 2))
                nc.scalar.activation(w_hi[:, u % 2, :], raw[:, u % 2, :], ACT.Copy).then_inc(w_hi_ready, 1)

            def finish(b, n, src, scale=1.0):
                chunk = POOL_ORDER[n] if b == 0 else n
                layer, g = GATES[b]
                if n >= 3:
                    act.wait_ge(xv_added if b < 3 else yy_added, (NC - 1) * (b if b < 3 else 4) + n - 2)
                to = sums if n == 0 else work[:, n % 2]
                nc.scalar.activation(to[:, 0, :], src, ACT.Square, scale=scale).then_inc(y_sq, 1)
                if b == 0:
                    nc.scalar.activation(y[:, chunk, :], src, ACT.Copy, scale=scale).then_inc(y_copied, 1)
                    act.wait_ge(y_copied, n + 1)
                    src = y[:, chunk, :]
                act.wait_ge(y_sq, NC * b + n + 1)
                act.wait_ge(mod_ready, GATE_MADE[b])
                nc.scalar.activation(y[:, chunk, :], src, ACT.Copy, scale=mod[:, layer, g, chunk:chunk + 1]).then_inc(v_ready, 1)
                if b < 3:
                    act.wait_ge(v_ready, NC * b + n + 1)
                    nc.scalar.activation(to[:, 2, :], y[:, chunk, :], ACT.Square).then_inc(v_sq, 1)

            def root(k):
                if k % 2:
                    act.wait_ge(yy_cols, k // 2 + 2)
                    to, src = rms_y, ps[:, Y_BANK, 0:NT]
                else:
                    act.wait_ge(xx_ready, k // 2 + 1)
                    to, src = rms_x, xx[:, :]
                nc.scalar.activation(to[:, 0, :], src, ACT.Sqrt, bias=eps[:, 0:1], scale=1.0 / D).then_inc(rms_ready, 1)

            def load_ada(q, units, slots):
                for i in units:
                    act.wait_ge(ada_used, q * ADA_Q + ADA_FIRST + (i + 1 - slots if i >= slots else 0))
                    seg, kk = i % LATER_SEGS, i // LATER_SEGS
                    rows = bass.ds(q * 2 * P + kk * P, P)
                    src = (ada_w[0, rows, GATE_F * D:(GATE_F + 1) * D] if seg == 0 else
                           ada_w[1, rows, (seg - 1) * D:seg * D])
                    act.dma_start(ada_raw[:, i % slots, :], src).then_inc(ada_in[i % slots], 16)

            def hidden(layer, q, j):
                for m in range(BANKS):
                    n = BANKS * (j // 2) + m
                    i = layer * QUARTERS * NC + n
                    act.wait_ge(bank_done, q * (BANKS * Q_UNITS // 2) + (NC + BANKS * pair(FFN_U[layer] + j) + m + 1))
                    if i >= 2:
                        act.wait_ge(hid_lo, q * NC + (i - 1))
                    nc.scalar.activation(relu[:, n % 2, :], ps[:, BANKS * (j // 2) + m, :], ACT.Relu).then_inc(relu_done, 1)
                    act.wait_ge(relu_done, q * NC + (i + 1))
                    nc.scalar.activation(mid_hi[:, n, :], relu[:, n % 2, :], ACT.Square).then_inc(hid_hi, 1)

            def mlp_quarter(layer, q, last=False):
                b = 1 + 2 * layer
                for j in range(Q_UNITS):
                    u = FFN_U[layer] + j
                    if last and layer == 0 and j == 0:
                        load_ada(q, (2,), 3)
                    if j == 3:
                        hidden(layer, q, j)
                    if last and j == 7:
                        for n in range(4, NC):
                            act.wait_ge(y_sum, NC * (QUARTERS * (layer + 1) - 1) + n + 1)
                            finish(b, n, y[:, n, :])
                    elif not (last and u + Q_UNITS * q + 2 >= UNITS):
                        split_hi(u + 2, q)
                    if j == 1:
                        hidden(layer, q, j)
                    if last and j == 5:
                        for n in range(4):
                            act.wait_ge(y_sum, NC * (QUARTERS * (layer + 1) - 1) + n + 1)
                            finish(b, n, y[:, n, :])
                    if layer == 0:
                        if last and j < Q_UNITS - 1:
                            load_ada(q, last_units(j + 1), 3)
                        elif not last and j + 1 < LATER_SEGS:
                            load_ada(q, (2 * j + 2, 2 * j + 3), 2)
                        elif not last and j + 1 == Q_UNITS:
                            load_ada(q + 1, (0, 1), 2)

            def boundary(b):
                root(2 * b + 1)
                if b == 3:
                    for half in range(2):
                        for j in range(NT - 2 * half):
                            act.wait_ge(out_turned, 4 * (half + 1))
                            nc.scalar.activation(x_tok[:, j, half * T:(half + 1) * T], ps[:, j, :], ACT.Copy).then_inc(out_by_act, 1)
                    return
                if b > 0:
                    split_hi(SECOND[b])
                root(2 * b + 2)
                if b == 0:
                    split_hi(1)
                layer, a = INPUTS[b]
                act.wait_ge(mod_ready, INPUT_MADE[b])
                for n in range(NC):
                    act.wait_ge(h_norm, NC * b + n + 1)
                    nc.scalar.activation(y[:, n, :], y[:, n, :], ACT.Identity, bias=mod[:, layer, a + 1, n:n + 1],
                                         scale=mod[:, layer, a, n:n + 1]).then_inc(h_full, 1)
                    act.wait_ge(h_full, NC * b + n + 1)
                    nc.scalar.activation(in_hi[:, n, :], y[:, n, :], ACT.Copy).then_inc(h_hi, 1)
                    if b == 0 and n == 3:
                        split_hi(2)

            act.wait_ge(vec_turned, 1)
            nc.scalar.activation(vec[:, :], ps[:, 5, 0:V_END], ACT.Copy).then_inc(vec_ready, 1)
            act.wait_ge(vec_ready, 1)
            nc.scalar.activation(silu_t[:, 0, :], vec[:, V_C:V_END], ACT.Exp, scale=-1.0).then_inc(exp_ready, 1)
            for n in range(NC):
                act.wait_ge(x_turned, n + 1)
                nc.scalar.activation(xs[:, n, :], ps[:, n % 4, :], ACT.Copy).then_inc(x_copied, 1)
                if n >= 3:
                    act.wait_ge(yy_added, n - 2)
                nc.scalar.activation(sums[:, 0, :] if n == 0 else work[:, n % 2, 0, :], ps[:, n % 4, :], ACT.Square).then_inc(x_sq, 1)
            act.wait_ge(eps_ready, 1)
            root(0)
            split_hi(POOL_U)
            for i in range(NC + 1):
                if i < NC:
                    n = POOL_ORDER[i]
                    act.wait_ge(mod_ready, 2)
                    act.wait_ge(mean_scale, 1)
                    act.wait_ge(window_ready, i // 2 + 1)
                    nc.scalar.activation(y[:, n, :], y[:, n, :], ACT.Identity, bias=mod[:, 0, 1, n:n + 1],
                                         scale=a_by_w[:, n:n + 1]).then_inc(pool_mean, 1)
                    nc.scalar.activation(norm0(n), norm0(n), ACT.Identity, bias=mod[:, 0, 1, n:n + 1],
                                         scale=mod[:, 0, 0, n:n + 1]).then_inc(pool_h, 1)
                if i >= 1:
                    n = POOL_ORDER[i - 1]
                    act.wait_ge(pool_diff, i)
                    nc.scalar.activation(in_hi[:, n, :], y[:, n, :], ACT.Copy).then_inc(h_hi, 1)
            for i in range(NC):
                act.wait_ge(bank_done, i + 1)
                finish(0, i, ps[:, POOL_BANK[i], :], col(V_POOL, POOL_ORDER[i]))
            boundary(0)
            load_ada(0, (0, 1), 2)
            with act.Fori(0, LOOP_Q) as q:
                mlp_quarter(0, q)
            mlp_quarter(0, LOOP_Q, last=True)
            boundary(1)
            for g in range(6):
                u = CONV_U + 2 * g
                split_hi(u + 2)
                if g in CV_GROUPS:
                    for p in (0, 1):
                        n = 2 * CV_GROUPS.index(g) + p
                        act.wait_ge(bank_done, NC + BANKS * pair(u) + 2 * p + 1)
                        if n >= 2:
                            act.wait_ge(cu_ready, n - 1)
                        nc.scalar.activation(cgate[:, p, :], ps[:, BANKS * (g % 2) + 2 * p, :], ACT.Copy).then_inc(c_copied, 1)
                        act.wait_ge(cu_ready, n + 1)
                        nc.scalar.activation(y[:, n, :], cu[:, p, 1:T + 1], ACT.Copy, scale=col(V_CONV + NC, n)).then_inc(z_mid, 1)
                else:
                    for m in range(BANKS):
                        n = BANKS * (g // 3) + m
                        act.wait_ge(gated, n + 1)
                        nc.scalar.activation(mid_hi[:, n, :], y[:, n, :], ACT.Copy).then_inc(g_hi, 1)
                split_hi(u + 3)
            for g in range(2):
                u = OUT_U + 2 * g
                split_hi(u + 2)
                for m in range(BANKS):
                    act.wait_ge(bank_done, NC + BANKS * pair(u) + m + 1)
                    finish(2, BANKS * g + m, ps[:, BANKS * g + m, :])
                if g == 0:
                    split_hi(u + 3)
            boundary(2)
            with act.Fori(0, LOOP_Q) as q:
                mlp_quarter(1, q)
            mlp_quarter(1, LOOP_Q, last=True)
            boundary(3)

        @block.vector
        def _(dve):
            def split_lo(u, q=0):
                dve.wait_ge(w_hi_ready, q * Q_UNITS + (u + 1))
                nc.vector.tensor_tensor(w_lo[:, u % 2, :], raw[:, u % 2, :], w_hi[:, u % 2, :].bitcast(F32), ALU.subtract).then_inc(w_lo_ready, 1)

            def first_ada(a):
                s, k = a // NC, a % NC
                dve.wait_ge(ada_in[a % ADA_SLOTS], 16 * (a // ADA_SLOTS + 1))
                if k:
                    dve.wait_ge(ada_used, a)
                    nc.vector.scalar_tensor_tensor(out=ada_sum[:, s, :], in0=ada_raw[:, a % ADA_SLOTS, :], scalar=silu_t[:, 3, k:k + 1],
                                                   in1=ada_sum[:, s, :], op0=ALU.mult, op1=ALU.add).then_inc(ada_used, 1)
                else:
                    nc.vector.tensor_scalar(ada_sum[:, s, :], ada_raw[:, a % ADA_SLOTS, :], silu_t[:, 3, 0:1], None, ALU.mult).then_inc(ada_used, 1)

            def later_ada(q, units, last):
                dve.wait_ge(sums_zero, 1)
                for i in units:
                    slots = 3 if last else 2
                    dve.wait_ge(ada_in[i % slots], (0 if last else q * (16 * LATER_SEGS)) + ada_landed(i, last))
                    dve.wait_ge(ada_used, q * ADA_Q + (ADA_FIRST + i - LATER_SEGS + 1))
                    k, s = q * 2 + i // LATER_SEGS, i % LATER_SEGS
                    nc.vector.scalar_tensor_tensor(out=ada_sum[:, s, :], in0=ada_raw[:, i % slots, :], scalar=silu_t[:, 3, bass.ds(k, 1)],
                                                   in1=ada_sum[:, s, :], op0=ALU.mult, op1=ALU.add).then_inc(ada_used, 1)

            made = [0]

            def make_mod(i):
                if i is None:
                    return
                _, layer, seg, bank = VECTORS[i]
                dve.wait_ge(ada_cols, i + 1)
                src = ps[:, bank, 0:NC]
                bias = vec[:, V_ADA_B + (layer * 6 + seg) * NC:V_ADA_B + (layer * 6 + seg + 1) * NC]
                mlp = seg >= SHIFT_F
                if seg in (SHIFT_M, SHIFT_F):
                    nc.vector.tensor_tensor(mod[:, layer, 3 * mlp + 1, :], src, bias, ALU.add).then_inc(mod_ready, 1)
                    return
                nc.vector.tensor_tensor(mod_t[:, layer, seg, :], src, bias, ALU.add).then_inc(mod_step, 1)
                made[0] += 1
                dve.wait_ge(mod_step, made[0])
                gate = seg in (GATE_M, GATE_F)
                g = V_NORM_G + (layer * 4 + 2 * mlp + gate) * NC
                nc.vector.scalar_tensor_tensor(out=mod[:, layer, 3 * mlp + 2 * gate, :], in0=mod_t[:, layer, seg, :],
                                               scalar=0.0 if gate else 1.0, in1=vec[:, g:g + NC], op0=ALU.add,
                                               op1=ALU.mult).then_inc(mod_ready, 1)

            def reciprocal_rms(k):
                rms, diag = (rms_y, diag_y) if k % 2 else (rms_x, diag_x)
                dve.wait_ge(rms_ready, k + 1)
                nc.vector.reciprocal(rms[:, 1, :], rms[:, 0, :]).then_inc(rcp_ready, 1)
                dve.wait_ge(rcp_ready, k + 1)
                for j in range(NT):
                    op = nc.vector.tensor_scalar(diag[:, j, :], ident[:, :], rms[:, 1, j:j + 1], None, ALU.mult)
                op.then_inc(diag_ready, 1)

            def add_squares(n, ready, value, before):
                dve.wait_ge(ready, value)
                add_wait(dve, yy_added, before)
                nc.vector.tensor_tensor(sums[:, 0, :], sums[:, 0, :], work[:, n % 2, 0, :], ALU.add).then_inc(yy_added, 1)

            def finish(b, n):
                chunk = POOL_ORDER[n] if b == 0 else n
                if n >= 1:
                    add_squares(n, y_sq, NC * b + n + 1, (NC - 1) * (b + 1) + n - 1)
                if b == 3:
                    return
                to = sums if n == 0 else work[:, n % 2]
                dve.wait_ge(v_ready, NC * b + n + 1)
                nc.vector.tensor_tensor(to[:, 1, :], xs[:, chunk, :], y[:, chunk, :], ALU.mult).then_inc(xv_ready, 1)
                if n >= 1:
                    dve.wait_ge(v_sq, NC * b + n + 1)
                    dve.wait_ge(xv_ready, NC * b + n + 1)
                    add_wait(dve, xv_added, (NC - 1) * b + n - 1)
                    nc.vector.tensor_tensor(sums[:, 1:3, :], sums[:, 1:3, :], work[:, n % 2, 1:3, :], ALU.add).then_inc(xv_added, 1)

            def new_xx(b):
                r = rms_y[:, 1, :]
                dve.wait_ge(xv_cols, b + 1)
                nc.vector.tensor_tensor(xx_t[:, 0, :], ps[:, XV_BANK, NT:2 * NT], r, ALU.mult).then_inc(xx_step, 1)
                dve.wait_ge(xx_step, 4 * b + 1)
                nc.vector.scalar_tensor_tensor(out=xx_t[:, 1, :], in0=ps[:, XV_BANK, 0:NT], scalar=2.0, in1=xx_t[:, 0, :],
                                               op0=ALU.mult, op1=ALU.add).then_inc(xx_step, 1)
                dve.wait_ge(xx_step, 4 * b + 2)
                nc.vector.tensor_tensor(xx_t[:, 2, :], xx_t[:, 1, :], r, ALU.mult).then_inc(xx_step, 1)
                dve.wait_ge(xx_step, 4 * b + 3)
                nc.vector.tensor_tensor(xx_t[:, 3, :], xx_t[:, 2, :], xx[:, :], ALU.add).then_inc(xx_step, 1)
                dve.wait_ge(xx_step, 4 * b + 4)
                nc.vector.tensor_scalar(xx[:, :], xx_t[:, 3, :], 0.0, None, ALU.max).then_inc(xx_ready, 1)

            def boundary(b):
                first, second, third = AT_BOUNDARY[b]
                reciprocal_rms(2 * b + 1)
                if b < 3:
                    make_mod(first)
                    make_mod(second)
                    new_xx(b)
                    reciprocal_rms(2 * b + 2)
                    make_mod(third)
                if b == 0:
                    split_lo(1)
                dve.wait_ge(bcast_done, 2 * b + 2)
                for i in range(NC + 4):
                    if i < NC:
                        nc.vector.tensor_tensor(y[:, i, :], y[:, i, :], ps[:, R_BANK, :], ALU.mult).then_inc(y_norm, 1)
                    if 1 <= i <= NC:
                        n = i - 1
                        dve.wait_ge(y_norm, NC * b + n + 1)
                        nc.vector.tensor_tensor(xs[:, n, :], xs[:, n, :], y[:, n, :], ALU.add).then_inc(x_new, 1)
                    if b == 3:
                        continue
                    if 2 <= i <= NC + 1:
                        n = i - 2
                        if n == 0:
                            dve.wait_ge(bcast_done, 2 * b + 3)
                        dve.wait_ge(x_new, NC * b + n + 1)
                        nc.vector.tensor_tensor(y[:, n, :], xs[:, n, :], ps[:, R2_BANK, :], ALU.mult).then_inc(h_norm, 1)
                    if i >= 4:
                        n = i - 4
                        dve.wait_ge(h_hi, NC * (b + 1) + n + 1)
                        nc.vector.tensor_tensor(in_lo[:, n, :], y[:, n, :], in_hi[:, n, :].bitcast(F32), ALU.subtract).then_inc(h_lo, 1)
                    if i == (9 if b == 0 else 6):
                        dve.wait_ge(w_lo_by_pool, b + 1)
                        nc.vector.tensor_copy(note[:, 1:2], note[:, 0:1]).then_inc(w_lo_ready, 1)
                if b == 3:
                    for j in (2, 3):
                        dve.wait_ge(out_turned, NC)
                        nc.vector.tensor_copy(x_tok[:, j, T:2 * T], ps[:, j, :]).then_inc(out_by_dve, 1)

            def hidden(layer, q, j):
                for m in range(BANKS):
                    n = BANKS * (j // 2) + m
                    i = layer * QUARTERS * NC + n
                    dve.wait_ge(hid_hi, q * NC + (i + 1))
                    nc.vector.tensor_tensor(relu[:, n % 2, :], relu[:, n % 2, :], relu[:, n % 2, :], ALU.mult).then_inc(hid_sq, 1)
                    dve.wait_ge(hid_sq, q * NC + (i + 1))
                    nc.vector.tensor_tensor(mid_lo[:, n, :], relu[:, n % 2, :], mid_hi[:, n, :].bitcast(F32), ALU.subtract).then_inc(hid_lo, 1)

            def mlp_quarter(layer, q, last=False):
                b = 1 + 2 * layer
                for j in range(Q_UNITS):
                    u = FFN_U[layer] + j
                    if j == 3:
                        hidden(layer, q, j)
                    if j in (5, 7):
                        dve.wait_ge(y_zero, layer + 1)
                        for m in range(BANKS):
                            n = BANKS * (j // 2 - 2) + m
                            dve.wait_ge(bank_done, q * (BANKS * Q_UNITS // 2) + (NC + BANKS * pair(u) + m + 1))
                            nc.vector.tensor_tensor(y[:, n, :], y[:, n, :], ps[:, BANKS * (j // 2 - 2) + m, :], ALU.add).then_inc(y_sum, 1)
                            if last and n > 4:
                                finish(b, n - 1)
                    if last and j == 7:
                        finish(b, NC - 1)
                    elif not (last and u + Q_UNITS * q + 2 >= UNITS):
                        split_lo(u + 2, q)
                    if j == 1:
                        hidden(layer, q, j)
                    if last and j == 5:
                        if layer == 0:
                            make_mod(5)
                        for n in range(4):
                            finish(b, n)
                    if layer == 0:
                        if last and LAST_STEPS[j]:
                            later_ada(q, last_units(j), True)
                        elif not last and j < LATER_SEGS:
                            later_ada(q, (2 * j, 2 * j + 1), False)

            nc.vector.memset(note[:, :], 0.0)
            dve.wait_ge(exp_ready, 1)
            nc.vector.tensor_scalar(silu_t[:, 1, :], silu_t[:, 0, :], 1.0, None, ALU.add).then_inc(silu_step, 1)
            dve.wait_ge(silu_step, 1)
            nc.vector.reciprocal(silu_t[:, 2, :], silu_t[:, 1, :]).then_inc(silu_step, 1)
            dve.wait_ge(silu_step, 2)
            nc.vector.tensor_tensor(silu_t[:, 3, :], silu_t[:, 2, :], vec[:, V_C:V_END], ALU.mult).then_inc(silu_step, 1)
            dve.wait_ge(silu_step, 3)

            for n in range(1, NC):
                add_squares(n, x_sq, n + 1, n - 1)
                if n >= 5:
                    first_ada(n - 5)
            dve.wait_ge(yy_cols, 1)
            nc.vector.tensor_copy(xx[:, :], ps[:, Y_BANK, 0:NT]).then_inc(xx_ready, 1)
            first_ada(3)
            reciprocal_rms(0)
            first_ada(4)
            dve.wait_ge(bcast_done, 1)
            for i, n in enumerate(POOL_ORDER):
                nc.vector.tensor_tensor(norm0(n), xs[:, n:n + 1, :], ps[:, R_BANK:R_BANK + 1, :], ALU.mult).then_inc(norm0_ready, 1)
                first_ada(5 + i)
            for a in range(13, 2 * NC):
                first_ada(a)
            make_mod(0)
            make_mod(1)
            dve.wait_ge(mod_ready, 2)
            for g, w in enumerate(WINDOWS):
                op = nc.vector.tensor_scalar(a_by_w[:, 2 * g:2 * g + 2], mod[:, 0, 0, 2 * g:2 * g + 2], 1.0 / w, None, ALU.mult)
            op.then_inc(mean_scale, 1)
            split_lo(POOL_U)
            at = 2 * NC
            for i in range(NC + 2):
                if 1 <= i <= NC:
                    n = POOL_ORDER[i - 1]
                    dve.wait_ge(pool_h, i)
                    nc.vector.tensor_tensor(y[:, n:n + 1, :], y[:, n:n + 1, :], norm0(n), ALU.subtract).then_inc(pool_diff, 1)
                if i >= 2:
                    n = POOL_ORDER[i - 2]
                    dve.wait_ge(h_hi, i - 1)
                    nc.vector.tensor_tensor(in_lo[:, n, :], y[:, n, :], in_hi[:, n, :].bitcast(F32), ALU.subtract).then_inc(h_lo, 1)
                first_ada(at)
                at += 1
                if at == 3 * NC + 1:
                    make_mod(2)
            for n in range(NC):
                finish(0, n)
                first_ada(at)
                at += 1
            while at < ADA_FIRST:
                first_ada(at)
                at += 1
            boundary(0)
            with dve.Fori(0, LOOP_Q) as q:
                mlp_quarter(0, q)
            mlp_quarter(0, LOOP_Q, last=True)
            boundary(1)
            dve.wait_ge(cu_pad, 1)
            for g in range(6):
                u = CONV_U + 2 * g
                split_lo(u + 2)
                if g in CV_GROUPS:
                    for p in (0, 1):
                        n = 2 * CV_GROUPS.index(g) + p
                        dve.wait_ge(bank_done, NC + BANKS * pair(u) + 2 * p + 2)
                        dve.wait_ge(c_copied, n + 1)
                        nc.vector.tensor_tensor(cu[:, p, 1:T + 1], cgate[:, p, :], ps[:, BANKS * (g % 2) + 2 * p + 1, :], ALU.mult).then_inc(cu_ready, 1)
                        dve.wait_ge(z_mid, n + 1)
                        nc.vector.scalar_tensor_tensor(out=y[:, n, :], in0=cu[:, p, 0:T], scalar=col(V_CONV, n), in1=y[:, n, :],
                                                       op0=ALU.mult, op1=ALU.add).then_inc(z_left, 1)
                        dve.wait_ge(z_left, n + 1)
                        nc.vector.scalar_tensor_tensor(out=y[:, n, :], in0=cu[:, p, 2:T + 2], scalar=col(V_CONV + 2 * NC, n), in1=y[:, n, :],
                                                       op0=ALU.mult, op1=ALU.add).then_inc(z_ready, 1)
                else:
                    for m in range(BANKS):
                        n = BANKS * (g // 3) + m
                        dve.wait_ge(bank_done, NC + BANKS * pair(u) + m + 1)
                        dve.wait_ge(z_ready, n + 1)
                        nc.vector.tensor_tensor(y[:, n, :], y[:, n, :], ps[:, BANKS * (g % 2) + m, :], ALU.mult).then_inc(gated, 1)
                        dve.wait_ge(g_hi, n + 1)
                        nc.vector.tensor_tensor(mid_lo[:, n, :], y[:, n, :], mid_hi[:, n, :].bitcast(F32), ALU.subtract).then_inc(g_lo, 1)
                split_lo(u + 3)
            for g in range(2):
                u = OUT_U + 2 * g
                split_lo(u + 2)
                for m in range(BANKS):
                    finish(2, BANKS * g + m)
                if g == 0:
                    split_lo(u + 3)
            boundary(2)
            with dve.Fori(0, LOOP_Q) as q:
                mlp_quarter(1, q)
            mlp_quarter(1, LOOP_Q, last=True)
            boundary(3)

        @block.gpsimd
        def _(pool):
            nc.gpsimd.memset(ident[:, :], 0.0).then_inc(ident_zero, 1)
            nc.gpsimd.memset(ones[:, :], 1.0).then_inc(consts_ready, 1)
            pool.wait_ge(ident_zero, 1)
            nc.gpsimd.affine_select(out=ident[:, :], in_=ident[:, :], compare_op=ALU.not_equal, fill=1.0, base=0,
                                    pattern=[[-1, P]], channel_multiplier=1).then_inc(consts_ready, 1)
            nc.gpsimd.memset(eps[:, :], EPS).then_inc(eps_ready, 1)
            steps = [0]

            def step(op):
                steps[0] += 1
                op.then_inc(level_step, 1)
                pool.wait_ge(level_step, steps[0])

            def split_lo(u):
                pool.wait_ge(w_hi_ready, u + 1)
                nc.gpsimd.tensor_tensor(w_lo[:, u % 2, :], raw[:, u % 2, :], w_hi[:, u % 2, :].bitcast(F32), ALU.subtract).then_inc(w_lo_by_pool, 1)

            at, edges = 0, []
            for w in WINDOWS:
                half = w // 2
                edges.append(at)
                for n in [t + half for t in range(half)] + [w - 1 - r for r in range(half - 1)]:
                    op = nc.gpsimd.memset(edge[:, :, at:at + 1], w / n)
                    at += 1
            step(op)
            for i in range(len(WINDOWS)):
                g = POOL_ORDER[2 * i] // 2
                w, at = WINDOWS[g], edges[g]
                half = w // 2
                t0, to = norm0(2 * g, 2), y[:, 2 * g:2 * g + 2, :]
                pool.wait_ge(norm0_ready, 2 * i + 2)
                if w == 2:
                    nc.gpsimd.tensor_copy(to[:, :, 0:1], t0[:, :, 0:1])
                    step(nc.gpsimd.tensor_tensor(to[:, :, 1:T], t0[:, :, 0:T - 1], t0[:, :, 1:T], ALU.add))
                else:
                    nc.gpsimd.memset(level[0][:, :, 0:PAD - 1], 0.0)
                    nc.gpsimd.memset(level[0][:, :, PAD + T:LEVEL], 0.0)
                    nc.gpsimd.tensor_copy(level[0][:, :, PAD - 1:PAD], t0[:, :, 0:1])
                    nc.gpsimd.tensor_copy(level[0][:, :, PAD + T - 1:PAD + T], t0[:, :, T - 1:T])
                    step(nc.gpsimd.tensor_tensor(level[0][:, :, PAD:PAD + T - 1], t0[:, :, 0:T - 1], t0[:, :, 1:T], ALU.add))
                    src, other, width, end = level[0], level[1], 2, LEVEL - 2
                    while 2 * width < w:
                        end -= width
                        step(nc.gpsimd.tensor_tensor(other[:, :, 0:end], src[:, :, 0:end], src[:, :, width:width + end], ALU.add))
                        src, other, width = other, src, 2 * width
                    lo = PAD - half
                    step(nc.gpsimd.tensor_tensor(to, src[:, :, lo:lo + T], src[:, :, lo + width:lo + width + T], ALU.add))
                    r = slice(T - half + 1, T)
                    step(nc.gpsimd.tensor_tensor(to[:, :, r], to[:, :, r], edge[:, :, at + half:at + w - 1], ALU.mult))
                nc.gpsimd.tensor_tensor(to[:, :, 0:half], to[:, :, 0:half], edge[:, :, at:at + half], ALU.mult).then_inc(window_ready, 1)
            pool.wait_ge(ada_cols, len(FIRST_SEGS))
            pool.wait_ge(pool_diff, NC)
            nc.gpsimd.memset(ada_sum[:, :, :], 0.0).then_inc(sums_zero, 1)
            split_lo(SECOND[0])
            pool.wait_ge(h_lo, 2 * NC)
            nc.gpsimd.memset(y[:, :, :], 0.0).then_inc(y_zero, 1)
            pool.wait_ge(ada_cols, 8)
            nc.gpsimd.memset(cu[:, :, 0:1], 0.0)
            nc.gpsimd.memset(cu[:, :, T + 1:T + 2], 0.0).then_inc(cu_pad, 1)
            split_lo(SECOND[1])
            split_lo(SECOND[2])
            pool.wait_ge(h_lo, 4 * NC)
            nc.gpsimd.memset(y[:, :, :], 0.0).then_inc(y_zero, 1)


_INS = ['x', 'c', 'ada_w', 'ada_b', 'norm_g', 'ffn_w1', 'ffn_w2', 'pool_w', 'pool_scale', 'conv_in_w', 'conv_w', 'conv_out_w']


def kernel(**inputs):
    import numpy as _np
    import concourse.bacc as _bacc
    from concourse import mybir as _mybir
    from concourse.bass_utils import run_bass_kernel_spmd as _run

    nc = _bacc.Bacc("TRN2", target_bir_lowering=False, num_devices=1)
    arrays, args = {}, []
    for name in _INS:
        a = _np.ascontiguousarray(inputs[name])
        arrays[f"in_{name}_dram"] = a
        args.append(nc.dram_tensor(f"in_{name}_dram", a.shape, _mybir.dt.from_np(a.dtype), kind="ExternalInput").ap())
    args.append(nc.dram_tensor("out_dram", (1, T, D), _mybir.dt.float32, kind="ExternalOutput").ap())
    trunk(nc, *args)
    r = _run(nc, [arrays], core_ids=[0])
    return r.results[0]["out_dram"]
```

```python
from contextlib import ExitStack

import concourse.bass as bass
from concourse import mybir

F32 = mybir.dt.float32
F32R = mybir.dt.float32r
ALU = mybir.AluOpType
ACT = mybir.ActivationFunctionType

P = 128
D = 1024
NC = D // P
T = 512
NT = T // P
FF = 4096
EPS = 1e-6
WINDOWS = (2, 4, 8, 16)
GROUP = D // len(WINDOWS)

UK, UN = 4, 512
BANKS = UN // P
QUARTERS = 4
QF = FF // QUARTERS
Q_UNITS = 8
POOL_U = 0
FFN_U = (1, 1 + 4 * Q_UNITS + 16)
CONV_U = 1 + 4 * Q_UNITS
OUT_U = CONV_U + 12
UNITS = FFN_U[1] + 4 * Q_UNITS
RAW_SLOTS = 2
CV_GROUPS = (0, 1, 3, 4)
CV_COLS = (0, 256, 128, 384)

SHIFT_M, SCALE_M, GATE_M, SHIFT_F, SCALE_F, GATE_F = range(6)
FIRST_SEGS = (SCALE_M, SHIFT_M, GATE_M, SCALE_F, SHIFT_F)
LATER_SEGS = 7
ADA_SLOTS = 3
ADA_FIRST = len(FIRST_SEGS) * NC
ADA_DVE = 3 * NC
ADA_Q = 2 * LATER_SEGS
LOOP_Q = QUARTERS - 1
LAST_STEPS = (3, 3, 3, 3, 2, 0, 0, 0)

ADA_ORDER = (*range(2 * NC), *range(ADA_DVE, ADA_DVE + 4), *range(2 * NC, ADA_DVE), *range(ADA_DVE + 4, ADA_FIRST))
Y_SLOTS = 2
ORDER_SLOTS = (0, 1, 2, 5, 6) + tuple(i % 5 if i < 4 * NC else i % 3 for i in range(5, ADA_FIRST))
FIRST_SLOTS = tuple(ORDER_SLOTS[ADA_ORDER.index(a)] for a in range(ADA_FIRST))

V_ADA_B = 0
V_NORM_G = 2 * 6 * NC
V_POOL = V_NORM_G + 2 * 4 * NC
V_CONV = V_POOL + NC
V_C = V_CONV + 3 * NC
V_END = V_C + NC

R_BANK, R2_BANK, Y_BANK, XV_BANK = 6, 5, (0, 7, 7, 7), (1, 4, 4)
ADA_STEPS = (4, 4, 4, 6, 7, 8, 10, 12, 16)
ROW_BANKS = (6, 3)


def trunk(nc, x, c, ada_w, ada_b, norm_g, ffn_w1, ffn_w2, pool_w, pool_scale, conv_in_w, conv_w, conv_out_w, out):
    with ExitStack() as ctx:
        def sb(name, shape, dt=F32):
            return ctx.enter_context(nc.sbuf_tensor(name, shape, dt))

        def sem(name):
            return ctx.enter_context(nc.semaphore(name))

        xs = sb("xs", [P, NC, T])
        in_hi = sb("in_hi", [P, NC, T], F32R)
        in_lo = sb("in_lo", [P, NC, T], F32R)
        mid_hi = sb("mid_hi", [P, NC, T], F32R)
        mid_lo = sb("mid_lo", [P, NC, T], F32R)
        y = sb("y", [P, NC, T])
        raw = sb("raw", [P, RAW_SLOTS, UK * UN])
        w_hi = sb("w_hi", [P, 2, UK * UN], F32R)
        w_lo = sb("w_lo", [P, 2, UK * UN], F32R)
        ada_raw = sb("ada_raw", [P, ADA_SLOTS, D])
        ada_sum = sb("ada_sum", [P, LATER_SEGS, D])
        work = sb("work", [P, 2, 3, T])
        sums = sb("sums", [P, 3, T])
        vec = sb("vec", [P, V_END])
        mod = sb("mod", [P, 2, 6, NC])
        mod_t = sb("mod_t", [P, 2, 6, NC])
        silu_t = sb("silu_t", [P, 4, NC])
        rms_y = sb("rms_y", [P, 2, NT])
        rms_x = sb("rms_x", [P, 2, NT])
        xx = sb("xx", [P, NT])
        xx_t = sb("xx_t", [P, 5, NT])
        ident = sb("ident", [P, P])
        ones = sb("ones", [P, P])
        eps = sb("eps", [P, 1])
        note = sb("note", [P, 2])
        a_by_w = sb("a_by_w", [P, NC])
        pool_gate = sb("pool_gate", [P, NC])
        ps = ctx.enter_context(nc.psum_tensor("ps", [P, 8, T], F32))

        x_tok = raw[:, :, :].rearrange("p s (j d) -> p (s j) d", d=D)
        relu = work[:, :, 0, :]
        vec_rows = work[:, 0, 0, 0:2 * P].rearrange("p (s n) -> p s n", s=2)
        diag_y = work[:, 0, 0, :].rearrange("p (j q) -> p j q", j=NT)
        diag_x = work[:, 0, 1, :].rearrange("p (j q) -> p j q", j=NT)
        xn_tok = ada_sum[:, 3:7, :]
        h_pool = work[:, :, 2, :]
        x_squares = work[:, :, 2, :]
        bands = sums[:, :, :].rearrange("p a t -> p (a t)").rearrange("p (g t) -> p g t", g=len(WINDOWS))
        ends = [work[:, e, 1, :].rearrange("p (g t) -> p g t", g=len(WINDOWS)) for e in range(2)]
        ada_row = ada_sum[0:1, 3:5, :]

        def ada_slot(a):
            s = FIRST_SLOTS[a]
            if s >= 5:
                return y[:, 2 * s - 6:2 * s - 4, :].rearrange("p a t -> p (a t)")
            return ada_raw[:, s, :] if s < ADA_SLOTS else raw[:, 1, (s - ADA_SLOTS) * D:(s - ADA_SLOTS + 1) * D]

        def ada_value(a):
            return 16 * ORDER_SLOTS[:ADA_ORDER.index(a) + 1].count(FIRST_SLOTS[a])

        flat = ada_sum[:, :, :].rearrange("p s d -> p (s d)")
        cgate = flat[:, 0:2 * T].rearrange("p (s t) -> p s t", s=2)
        cu = flat[:, 2 * T:2 * T + 2 * (T + 2)].rearrange("p (s t) -> p s t", s=2)

        vec_in, out_done = sem("vec_in"), sem("out_done")
        x_in = [sem(f"x_in{j}") for j in range(NT)]
        raw_in = [sem(f"raw_in{s}") for s in range(RAW_SLOTS)]
        ada_in = [sem(f"ada_in{s}") for s in range(max(FIRST_SLOTS) + 1)]
        consts_ready, ident_zero, eps_ready = sem("consts_ready"), sem("ident_zero"), sem("eps_ready")
        vec_turned, vec_ready = sem("vec_turned"), sem("vec_ready")
        exp_ready, silu_step = sem("exp_ready"), sem("silu_step")
        x_turned, x_copied = sem("x_turned"), sem("x_copied")
        w_hi_ready, w_lo_ready, w_lo_by_pool = sem("w_hi_ready"), sem("w_lo_ready"), sem("w_lo_by_pool")
        unit_done, bank_done = sem("unit_done"), sem("bank_done")
        ada_used, ada_cols, mod_step, mod_ready, sums_zero = sem("ada_used"), sem("ada_cols"), sem("mod_step"), sem("mod_ready"), sem("sums_zero")
        bands_step, bands_ready = sem("bands_step"), sem("bands_ready")
        xn_ready, xn_turned, windowed, window_copied = sem("xn_ready"), sem("xn_turned"), sem("windowed"), sem("window_copied")
        ada_rows, row_copied = sem("ada_rows"), sem("row_copied")
        mean_scale = sem("mean_scale")
        pool_mean, pool_h, pool_diff = sem("pool_mean"), sem("pool_h"), sem("pool_diff")
        relu_done, hid_hi, hid_sq, hid_lo = sem("relu_done"), sem("hid_hi"), sem("hid_sq"), sem("hid_lo")
        y_zero, y_sum, pool_gate_ready = sem("y_zero"), sem("y_sum"), sem("pool_gate_ready")
        y_sq, v_ready, v_sq = sem("y_sq"), sem("v_ready"), sem("v_sq")
        yy_added, xv_ready, xv_added, x_sq = sem("yy_added"), sem("xv_ready"), sem("xv_added"), sem("x_sq")
        yy_cols, xv_cols, xx_step, xx_ready = sem("yy_cols"), sem("xv_cols"), sem("xx_step"), sem("xx_ready")
        rms_ready, rcp_ready, diag_ready, bcast_done = sem("rms_ready"), sem("rcp_ready"), sem("diag_ready"), sem("bcast_done")
        y_norm, x_new = sem("y_norm"), sem("x_new")
        h_norm, h_full, h_hi, h_lo = sem("h_norm"), sem("h_full"), sem("h_hi"), sem("h_lo")
        c_copied, cu_ready, cu_pad = sem("c_copied"), sem("cu_ready"), sem("cu_pad")
        z_mid, z_left, z_ready = sem("z_mid"), sem("z_left"), sem("z_ready")
        gated, g_hi, g_lo = sem("gated"), sem("g_hi"), sem("g_lo")
        x_back, x_back_copied = sem("x_back"), sem("x_back_copied")
        out_turned, out_made = sem("out_turned"), sem("out_made")

        block = ctx.enter_context(nc.Block())

        def pair(u):
            return (u - 1) // 2

        def unit_wait(eng, first, pairs):
            if first:
                eng.wait_ge(unit_done, pairs + 1)
            else:
                eng.wait_ge(bank_done, NC + BANKS * (pairs + 1))

        def raw_value(u):
            n = 0
            for v in range(u % 2, u + 1, 2):
                n += 32 if CONV_U <= v < OUT_U and (v - CONV_U) // 2 in CV_GROUPS else 16
            return n

        def col(base, chunk):
            return vec[:, base + chunk:base + chunk + 1]

        GATES = ((0, 2), (0, 5), (1, 2), (1, 5))
        INPUTS = ((0, 3), (1, 0), (1, 3))
        VECTORS = ((0, 0, SCALE_M, 0), (1, 0, SHIFT_M, 1),
                   (2, 0, GATE_M, 5),
                   (None, 0, SCALE_F, 2), (None, 0, SHIFT_F, 7),
                   (0, 0, GATE_F, 0),
                   (1, 1, SHIFT_M, 1), (2, 1, SCALE_M, 2), (3, 1, GATE_M, 3),
                   (4, 1, SHIFT_F, 1), (5, 1, SCALE_F, 2), (6, 1, GATE_F, 3))
        AT_BOUNDARY = ((3, 4, None), (6, 7, 8), (9, 10, 11))
        GATE_MADE = (3, 6, 9, 12)
        INPUT_MADE = (5, 8, 11)
        SECOND = (None, CONV_U + 1, FFN_U[1] + 1)

        def add_wait(eng, sem_x, value):
            if isinstance(value, int) and value <= 0:
                return
            eng.wait_ge(sem_x, value)

        def split_wait(eng, u, q=0):
            eng.wait_ge(w_lo_ready, q * Q_UNITS + (u + 1))

        def ada_landed(i, last):
            n = [FIRST_SLOTS.count(s) for s in range(ADA_SLOTS)]
            if last:
                return 16 * (n[i % 3] + (LOOP_Q * LATER_SEGS if i % 3 < 2 else 0) + i // 3 + 1)
            return 16 * (n[i % 2] + i // 2 + 1)

        def last_units(j):
            at = sum(LAST_STEPS[:j])
            return range(at, at + LAST_STEPS[j])

        def raw_cols(slot, cols=slice(0, UN)):
            return raw[:, slot, :].rearrange("p (k n) -> p k n", k=UK)[:, :, cols]

        def w_rows(w):
            return w.rearrange("(k p) n -> p k n", p=P)

        @block.sync
        def _(sp):
            sp.dma_start(vec_rows[0:V_NORM_G, 0, :], ada_b.rearrange("l (r p) -> (l r) p", p=P)).then_inc(vec_in, 16)
            at = 0
            for v, n in ((norm_g.rearrange("l g (r p) -> (l g r) p", p=P), V_POOL - V_NORM_G),
                         (pool_scale.rearrange("l (r p) -> (l r) p", p=P), NC),
                         (conv_w.rearrange("l w (r p) -> (l w r) p", p=P), 3 * NC),
                         (c.rearrange("l (r p) -> (l r) p", p=P), NC)):
                sp.dma_start(vec_rows[at:at + n, 1, :], v).then_inc(vec_in, 16)
                at += n
            for j in range(NT):
                sp.dma_start(x_tok[:, j, :], x[0, j * P:(j + 1) * P, :]).then_inc(x_in[j], 16)

            def load_ada(i):
                a = ADA_ORDER[i]
                if ORDER_SLOTS[i] in ORDER_SLOTS[:i]:
                    before = ADA_ORDER[max(b for b in range(i) if ORDER_SLOTS[b] == ORDER_SLOTS[i])]
                    if before >= ADA_DVE:
                        sp.wait_ge(ada_rows, before - ADA_DVE + 1)
                    else:
                        sp.wait_ge(ada_used, before + 1)
                seg, k = FIRST_SEGS[a // NC], a % NC
                sp.dma_start(ada_slot(a), ada_w[0, k * P:(k + 1) * P, seg * D:(seg + 1) * D]).then_inc(ada_in[FIRST_SLOTS[a]], 16)

            def load_mlp(layer, q, j):
                u = FFN_U[layer] + j
                if u > 1 or not isinstance(q, int):
                    sp.wait_ge(w_lo_ready, q * Q_UNITS + (u - 1))
                if j < 4:
                    src = ffn_w1[layer, (j % 2) * UK * P:(j % 2 + 1) * UK * P,
                                 bass.ds(q * QF + (j // 2) * UN, UN)]
                else:
                    src = ffn_w2[layer, bass.ds(q * QF + (j % 2) * UK * P, UK * P),
                                 (j // 2 - 2) * UN:(j // 2 - 1) * UN]
                sp.dma_start(raw_cols(u % 2), w_rows(src)).then_inc(raw_in[u % 2], 16)

            for a in range(ADA_SLOTS + Y_SLOTS):
                load_ada(a)
            sp.wait_ge(x_turned, NC)
            sp.wait_ge(x_sq, NT)
            sp.wait_ge(xn_ready, NT)
            for a in range(ADA_SLOTS + Y_SLOTS, 2 * NC):
                load_ada(a)
            sp.dma_start(raw[:, 0, :].rearrange("p (g n) -> p g n", g=2 * len(WINDOWS)),
                         pool_w[0].rearrange("g (k p) n -> p (g k) n", p=P)).then_inc(raw_in[0], 16)
            for a in range(2 * NC, 4 * NC + 2):
                load_ada(a)
            sp.wait_ge(ada_rows, max(a for a in ADA_ORDER[:4 * NC] if FIRST_SLOTS[a] >= ADA_SLOTS) - ADA_DVE + 1)
            load_mlp(0, 0, 0)
            for a in range(4 * NC + 2, ADA_FIRST):
                load_ada(a)
            with sp.Fori(0, LOOP_Q) as q:
                for j in range(1, Q_UNITS):
                    load_mlp(0, q, j)
                load_mlp(0, q + 1, 0)
            for j in range(1, Q_UNITS):
                load_mlp(0, LOOP_Q, j)
            for u in range(CONV_U, FFN_U[1]):
                split_wait(sp, u - 2)
                if u < OUT_U:
                    g, kk = (u - CONV_U) // 2, (u - CONV_U) % 2
                    rows = conv_in_w[0, kk * UK * P:(kk + 1) * UK * P, :]
                    if g in CV_GROUPS:
                        n = CV_GROUPS.index(g) * UN // 2
                        for i in (0, 1):
                            sp.dma_start(raw_cols(u % 2, slice(i * UN // 2, (i + 1) * UN // 2)),
                                         w_rows(rows[:, (1 + i) * D + n:(1 + i) * D + n + UN // 2])).then_inc(raw_in[u % 2], 16)
                    else:
                        n = (g // 3) * UN
                        sp.dma_start(raw_cols(u % 2), w_rows(rows[:, n:n + UN])).then_inc(raw_in[u % 2], 16)
                else:
                    g, kk = (u - OUT_U) // 2, (u - OUT_U) % 2
                    sp.dma_start(raw_cols(u % 2), w_rows(conv_out_w[0, kk * UK * P:(kk + 1) * UK * P,
                                                                    g * UN:(g + 1) * UN])).then_inc(raw_in[u % 2], 16)
            with sp.Fori(0, QUARTERS) as q:
                for j in range(Q_UNITS):
                    load_mlp(1, q, j)
            for half in range(2):
                for j in range(NT):
                    sp.wait_ge(out_made, half * NT + j + 1)
                    sp.dma_start(out[0, j * P:(j + 1) * P, half * T:(half + 1) * T],
                                 x_tok[:, j, half * T:(half + 1) * T]).then_inc(out_done, 16)
            sp.wait_ge(out_done, 16 * 2 * NT)

        @block.tensor
        def _(pe):
            def multiply(u, q, hi, lo, chunks, need, rows_first=False, cols=None):
                first = (u - 1) % 2 == 0
                banks = [BANKS * (pair(u) % 2) + m for m in range(BANKS)]
                cols = cols or [m * P for m in range(BANKS)]
                split_wait(pe, u, q)

                def products(kk, m):
                    n = kk * UN + cols[m]
                    a, b = w_hi[:, u % 2, n:n + P], w_lo[:, u % 2, n:n + P]
                    o = ps[:, banks[m], :]
                    nc.tensor.matmul(o, a, hi[:, chunks[kk], :], start=first and kk == 0, stop=False)
                    nc.tensor.matmul(o, a, lo[:, chunks[kk], :], start=False, stop=False)
                    return nc.tensor.matmul(o, b, hi[:, chunks[kk], :], start=False, stop=not first and kk == UK - 1)

                if first or rows_first:
                    for kk in range(UK):
                        need(kk)
                        for m in range(BANKS):
                            last = products(kk, m)
                            if not first and kk == UK - 1:
                                last.then_inc(bank_done, 1)
                    if first:
                        last.then_inc(unit_done, 1)
                else:
                    need(UK - 1)
                    for m in range(BANKS):
                        for kk in range(UK):
                            last = products(kk, m)
                        last.then_inc(bank_done, 1)

            def mlp_unit(layer, q, j):
                u = FFN_U[layer] + j
                half = UK * (j % 2)
                chunks = [half + kk for kk in range(UK)]
                if j < 4:
                    multiply(u, q, in_hi, in_lo, chunks,
                             lambda kk, n=NC * (1 + 2 * layer) + half: pe.wait_ge(h_lo, n + kk + 1), rows_first=j == 1)
                else:
                    multiply(u, q, mid_hi, mid_lo, chunks,
                             lambda kk, n=layer * QUARTERS * NC + half: pe.wait_ge(hid_lo, q * NC + (n + kk + 1)))

            def stat_cols(bank, at, src):
                for j in range(NT):
                    mm = nc.tensor.matmul(ps[:, bank, at + j:at + j + 1], src[:, j * P:(j + 1) * P], ones[:, 0:1],
                                          start=True, stop=True)
                return mm

            def broadcast(k):
                pe.wait_ge(diag_ready, k)
                nc.tensor.matmul(ps[:, R_BANK if k % 2 else R2_BANK, :], ones[:, :], diag_y if k % 2 else diag_x,
                                 start=True, stop=True).then_inc(bcast_done, 1)

            def reduce_vector(i):
                s, _, _, bank = VECTORS[i]
                if s is None:
                    pe.wait_ge(row_copied, 2 * (i - 3) + 2)
                    for m in range(NC):
                        mm = nc.tensor.matmul(ps[:, bank, m:m + 1], ada_row[:, i - 3, m * P:(m + 1) * P], ones[0:1, 0:1],
                                              start=True, stop=True)
                    mm.then_inc(ada_cols, 1)
                    return
                pe.wait_ge(ada_used, NC * (i + 1) if i < 3 else ADA_DVE + QUARTERS * ADA_Q)
                for m in range(NC):
                    mm = nc.tensor.matmul(ps[:, bank, m:m + 1], ada_sum[:, s, m * P:(m + 1) * P], ones[:, 0:1],
                                          start=True, stop=True)
                mm.then_inc(ada_cols, 1)

            def ada_unit(a):
                i, k = a // NC - 3, a % NC
                pe.wait_ge(ada_in[FIRST_SLOTS[a]], ada_value(a))
                for half in range(2):
                    mm = nc.tensor.matmul(ps[0:1, ROW_BANKS[i] + half, :], silu_t[:, 3, k:k + 1],
                                          ada_slot(a)[:, half * T:(half + 1) * T], start=k == 0, stop=k == NC - 1)
                mm.then_inc(ada_rows, 1)

            def keep_warm(bank, count):
                for _ in range(count):
                    nc.tensor.matmul(ps[:, bank, 0:P], ones[:, :], ident[:, :], start=True, stop=True)

            def boundary(b):
                if b in (1, 2):
                    if b == 1:
                        pe.wait_ge(y_sum, NC * (QUARTERS - 1) + 4)
                    else:
                        pe.wait_ge(v_ready, NC * b + 4)
                    for i in AT_BOUNDARY[b]:
                        reduce_vector(i)
                    pe.wait_ge(mod_ready, GATE_MADE[b])
                pe.wait_ge(v_ready, NC * (b + 1))
                pe.wait_ge(yy_added, (NC - 1) * (b + 1))
                stat_cols(Y_BANK[b], 0, sums[:, 0, :]).then_inc(yy_cols, 1)
                pe.wait_ge(xv_added, (NC - 1) * (b + 1))
                stat_cols(XV_BANK[b], 0, sums[:, 1, :])
                stat_cols(XV_BANK[b], NT, sums[:, 2, :]).then_inc(xv_cols, 1)
                broadcast(2 * b + 1)
                if b == 0:
                    reduce_vector(4)
                else:
                    keep_warm(0, 8)
                broadcast(2 * b + 2)
                keep_warm(0 if b else 3, 8)

            def turn_block(bank, src, half, j):
                for i in range(NC // 2):
                    tr = nc.tensor.transpose(ps[:, bank, i * P:(i + 1) * P], src[:, half * NC // 2 + i, j * P:(j + 1) * P], ident[:, :])
                return tr

            def result():
                pe.wait_ge(y_sum, NC * (2 * QUARTERS - 1) + 4)
                for j in range(NT):
                    turn_block(j, xs, 0, j).then_inc(x_back, 1)
                pe.wait_ge(v_ready, NC * 4)
                pe.wait_ge(yy_added, (NC - 1) * 4)
                stat_cols(Y_BANK[3], 0, sums[:, 0, :]).then_inc(yy_cols, 1)
                for half in range(2):
                    for j in range(NT):
                        if half == 1:
                            pe.wait_ge(x_back_copied, j + 1)
                            turn_block(j, xs, 1, j).then_inc(x_back, 1)
                            pe.wait_ge(out_made, j + 1)
                        elif j == Y_BANK[3] - NT:
                            pe.wait_ge(rms_ready, 8)
                        turn_block(NT + j, y, half, j).then_inc(out_turned, 1)

            pe.wait_ge(consts_ready, 2)
            pe.wait_ge(vec_in, 16 * 5)
            for s, (n, at) in enumerate(((V_NORM_G, 0), (V_END - V_NORM_G, V_NORM_G))):
                tr = nc.tensor.transpose(ps[:, 5, at:at + n], vec_rows[0:n, s, :], ident[0:n, 0:n])
            tr.then_inc(vec_turned, 1)
            for j in range(NT):
                pe.wait_ge(x_in[j], 16)
            for n in range(NC):
                if n >= 4:
                    pe.wait_ge(x_copied, n - 3)
                for j in range(NT):
                    tr = nc.tensor.transpose(ps[:, n % 4, j * P:(j + 1) * P], x_tok[:, j, n * P:(n + 1) * P], ident[:, :])
                tr.then_inc(x_turned, 1)
            pe.wait_ge(xn_ready, NT)
            pe.wait_ge(bands_ready, 1)
            for n in range(NC):
                g = n // 2
                if n >= 2:
                    pe.wait_ge(window_copied, n - 1)
                for j in range(NT):
                    own = ends[0][:, g, :] if j == 0 else ends[1][:, g, :] if j == NT - 1 else bands[:, g, P:2 * P]
                    parts = [(j, own)]
                    if j > 0:
                        parts.append((j - 1, bands[:, g, 2 * P:3 * P]))
                    if j < NT - 1 and WINDOWS[g] > 2:
                        parts.append((j + 1, bands[:, g, 0:P]))
                    for i, (src, table) in enumerate(parts):
                        mm = nc.tensor.matmul(ps[:, 6 + n % 2, j * P:(j + 1) * P], xn_tok[:, src, n * P:(n + 1) * P], table,
                                              start=i == 0, stop=i == len(parts) - 1)
                mm.then_inc(windowed, 1)
                if n == 5:
                    pe.wait_ge(x_copied, NC)
                    reduce_vector(0)

            def turn_xn(n):
                if n >= 2:
                    pe.wait_ge(pool_h, n - 1)
                for j in range(NT):
                    tr = nc.tensor.transpose(ps[:, 3 + n % 2, j * P:(j + 1) * P], xn_tok[:, j, n * P:(n + 1) * P], ident[:, :])
                tr.then_inc(xn_turned, 1)

            turn_xn(0)
            turn_xn(1)
            reduce_vector(1)
            pe.wait_ge(window_copied, NC)
            ada_unit(ADA_DVE)
            turn_xn(2)
            ada_unit(ADA_DVE + 1)
            turn_xn(3)
            ada_unit(ADA_DVE + 2)
            ada_unit(ADA_DVE + 3)
            pe.wait_ge(w_lo_ready, 1)
            for n in range(NC):
                if n < 2:
                    turn_xn(2 * n + 4)
                    turn_xn(2 * n + 5)
                if n == 3:
                    reduce_vector(2)
                if n >= 3:
                    pe.wait_ge(v_ready, n - 2)
                g, bank = n // 2, ps[:, n % 3, :]
                for kk in range(2):
                    pe.wait_ge(h_lo, 2 * g + kk + 1)
                    at = (2 * g + kk) * GROUP + (n % 2) * P
                    a, b = w_hi[:, 0, at:at + P], w_lo[:, 0, at:at + P]
                    nc.tensor.matmul(bank, a, in_hi[:, 2 * g + kk, :], start=kk == 0, stop=False)
                    nc.tensor.matmul(bank, a, in_lo[:, 2 * g + kk, :], start=False, stop=False)
                    mm = nc.tensor.matmul(bank, b, in_hi[:, 2 * g + kk, :], start=False, stop=kk == 1)
                mm.then_inc(bank_done, 1)
                for a in range(ADA_STEPS[n], ADA_STEPS[n + 1]):
                    ada_unit(ADA_DVE + a)
                if n == NC - 1:
                    reduce_vector(3)
            boundary(0)
            with pe.Fori(0, LOOP_Q) as q:
                for j in range(Q_UNITS):
                    mlp_unit(0, q, j)
            for j in range(Q_UNITS):
                if j == 6:
                    pe.wait_ge(y_sum, NC * LOOP_Q + 1)
                    reduce_vector(5)
                mlp_unit(0, LOOP_Q, j)
            boundary(1)
            for g in range(6):
                for kk in (0, 1):
                    multiply(CONV_U + 2 * g + kk, 0, in_hi, in_lo, [UK * kk + i for i in range(UK)],
                             lambda i, n=NC * 2 + UK * kk: pe.wait_ge(h_lo, n + i + 1), rows_first=g == 0,
                             cols=CV_COLS if g in CV_GROUPS else None)
            for g in range(2):
                for kk in (0, 1):
                    multiply(OUT_U + 2 * g + kk, 0, mid_hi, mid_lo, [UK * kk + i for i in range(UK)],
                             lambda i, n=UK * kk: pe.wait_ge(g_lo, n + i + 1))
            boundary(2)
            with pe.Fori(0, QUARTERS) as q:
                for j in range(Q_UNITS):
                    mlp_unit(1, q, j)
            result()

        @block.scalar
        def _(act):
            def split_hi(u, q=0):
                raw_at = raw_value(u + Q_UNITS * q) if isinstance(q, int) else q * (16 * Q_UNITS // 2) + raw_value(u)
                act.wait_ge(raw_in[u % 2], raw_at)
                if u == 2:
                    act.wait_ge(bank_done, NC)
                elif u > 2:
                    unit_wait(act, (u - 3) % 2 == 0, q * (Q_UNITS // 2) + pair(u - 2))
                nc.scalar.activation(w_hi[:, u % 2, :], raw[:, u % 2, :], ACT.Copy).then_inc(w_hi_ready, 1)

            def finish(b, n, src):
                layer, g = GATES[b]
                if n >= 3:
                    act.wait_ge(xv_added if b < 3 else yy_added, (NC - 1) * b + n - 2)
                to = sums if n == 0 else work[:, n % 2]
                if b == 0:
                    nc.scalar.activation(to[:, 0, :], src, ACT.Square, scale=col(V_POOL, n)).then_inc(y_sq, 1)
                    act.wait_ge(pool_gate_ready, 1)
                    gate = pool_gate[:, n:n + 1]
                else:
                    nc.scalar.activation(to[:, 0, :], src, ACT.Square).then_inc(y_sq, 1)
                    act.wait_ge(y_sq, NC * b + n + 1)
                    act.wait_ge(mod_ready, GATE_MADE[b])
                    gate = mod[:, layer, g, n:n + 1]
                nc.scalar.activation(y[:, n, :], src, ACT.Copy, scale=gate).then_inc(v_ready, 1)
                if b < 3:
                    act.wait_ge(v_ready, NC * b + n + 1)
                    nc.scalar.activation(to[:, 2, :], y[:, n, :], ACT.Square).then_inc(v_sq, 1)

            def root(k):
                if k % 2:
                    act.wait_ge(yy_cols, k // 2 + 1)
                    to, src = rms_y, ps[:, Y_BANK[k // 2], 0:NT]
                else:
                    if k == 0:
                        act.wait_ge(x_sq, NT)
                    else:
                        act.wait_ge(xx_ready, k // 2)
                    to, src = rms_x, xx[:, :]
                nc.scalar.activation(to[:, 0, :], src, ACT.Sqrt, bias=eps[:, 0:1], scale=1.0 / D).then_inc(rms_ready, 1)

            def load_ada(q, units, slots):
                for i in units:
                    act.wait_ge(ada_used, q * ADA_Q + ADA_DVE + (i + 1 - slots if i >= slots else 0))
                    seg, kk = i % LATER_SEGS, i // LATER_SEGS
                    rows = bass.ds(q * 2 * P + kk * P, P)
                    src = (ada_w[0, rows, GATE_F * D:(GATE_F + 1) * D] if seg == 0 else
                           ada_w[1, rows, (seg - 1) * D:seg * D])
                    act.dma_start(ada_raw[:, i % slots, :], src).then_inc(ada_in[i % slots], 16)

            def hidden(layer, q, j):
                for m in range(BANKS):
                    n = BANKS * (j // 2) + m
                    i = layer * QUARTERS * NC + n
                    act.wait_ge(bank_done, q * (BANKS * Q_UNITS // 2) + (NC + BANKS * pair(FFN_U[layer] + j) + m + 1))
                    if i >= 2:
                        act.wait_ge(hid_lo, q * NC + (i - 1))
                    nc.scalar.activation(relu[:, n % 2, :], ps[:, BANKS * (j // 2) + m, :], ACT.Relu).then_inc(relu_done, 1)
                    act.wait_ge(relu_done, q * NC + (i + 1))
                    nc.scalar.activation(mid_hi[:, n, :], relu[:, n % 2, :], ACT.Square).then_inc(hid_hi, 1)

            def mlp_quarter(layer, q, last=False):
                b = 1 + 2 * layer
                for j in range(Q_UNITS):
                    u = FFN_U[layer] + j
                    if last and layer == 0 and j == 0:
                        load_ada(q, (2,), 3)
                    if j == 3:
                        hidden(layer, q, j)
                    if last and j == 7:
                        for n in range(4, NC):
                            act.wait_ge(y_sum, NC * (QUARTERS * (layer + 1) - 1) + n + 1)
                            finish(b, n, y[:, n, :])
                    elif not (last and u + Q_UNITS * q + 2 >= UNITS):
                        split_hi(u + 2, q)
                    if j == 1:
                        hidden(layer, q, j)
                    if last and j == 5:
                        for n in range(4):
                            act.wait_ge(y_sum, NC * (QUARTERS * (layer + 1) - 1) + n + 1)
                            finish(b, n, y[:, n, :])
                    if layer == 0:
                        if last and j < Q_UNITS - 1:
                            load_ada(q, last_units(j + 1), 3)
                        elif not last and j + 1 < LATER_SEGS:
                            load_ada(q, (2 * j + 2, 2 * j + 3), 2)
                        elif not last and j + 1 == Q_UNITS:
                            load_ada(q + 1, (0, 1), 2)

            def boundary(b):
                root(2 * b + 1)
                if b == 0:
                    copy_row(1)
                else:
                    split_hi(SECOND[b])
                root(2 * b + 2)
                layer, a = INPUTS[b]
                act.wait_ge(mod_ready, INPUT_MADE[b])
                for n in range(NC):
                    act.wait_ge(h_norm, NC * b + n + 1)
                    nc.scalar.activation(y[:, n, :], y[:, n, :], ACT.Identity, bias=mod[:, layer, a + 1, n:n + 1],
                                         scale=mod[:, layer, a, n:n + 1]).then_inc(h_full, 1)
                    act.wait_ge(h_full, NC * b + n + 1)
                    nc.scalar.activation(in_hi[:, n, :], y[:, n, :], ACT.Copy).then_inc(h_hi, 1)
                    if b == 0 and n == 1:
                        split_hi(2)

            def copy_row(i):
                act.wait_ge(ada_rows, NC * (i + 1))
                for half in range(2):
                    nc.scalar.activation(ada_row[:, i, half * T:(half + 1) * T], ps[0:1, ROW_BANKS[i] + half, :],
                                         ACT.Copy).then_inc(row_copied, 1)

            act.wait_ge(vec_turned, 1)
            nc.scalar.activation(vec[:, :], ps[:, 5, 0:V_END], ACT.Copy).then_inc(vec_ready, 1)
            act.wait_ge(vec_ready, 1)
            nc.scalar.activation(silu_t[:, 0, :], vec[:, V_C:V_END], ACT.Exp, scale=-1.0).then_inc(exp_ready, 1)
            act.wait_ge(eps_ready, 1)
            for j in range(NT):
                act.wait_ge(x_in[j], 16)
                if j > 0:
                    act.wait_ge(x_sq, j)
                nc.scalar.activation(x_squares, x_tok[:, j, :].rearrange("p (a t) -> p a t", a=2), ACT.Square,
                                     accum_out=xx[:, j:j + 1]).then_inc(x_sq, 1)
            root(0)
            for n in range(NC):
                act.wait_ge(x_turned, n + 1)
                nc.scalar.activation(xs[:, n, :], ps[:, n % 4, :], ACT.Copy).then_inc(x_copied, 1)
            for n in range(NC):
                act.wait_ge(windowed, n + 1)
                if n == NC - 2 * Y_SLOTS:
                    act.wait_ge(ada_used, ADA_SLOTS + Y_SLOTS)
                nc.scalar.activation(y[:, n, :], ps[:, 6 + n % 2, :], ACT.Copy).then_inc(window_copied, 1)
            split_hi(POOL_U)
            act.wait_ge(mod_ready, 2)
            act.wait_ge(mean_scale, 1)
            for i in range(NC + 1):
                if i < NC:
                    act.wait_ge(window_copied, i + 1)
                    nc.scalar.activation(y[:, i, :], y[:, i, :], ACT.Identity, bias=mod[:, 0, 1, i:i + 1],
                                         scale=a_by_w[:, i:i + 1]).then_inc(pool_mean, 1)
                    act.wait_ge(xn_turned, i + 1)
                    if i >= 2:
                        act.wait_ge(pool_diff, i - 1)
                    nc.scalar.activation(h_pool[:, i % 2, :], ps[:, 3 + i % 2, :], ACT.Identity, bias=mod[:, 0, 1, i:i + 1],
                                         scale=mod[:, 0, 0, i:i + 1]).then_inc(pool_h, 1)
                if i >= 1:
                    n = i - 1
                    act.wait_ge(pool_diff, i)
                    nc.scalar.activation(in_hi[:, n, :], y[:, n, :], ACT.Copy).then_inc(h_hi, 1)
            for i in range(NC):
                act.wait_ge(bank_done, i + 1)
                finish(0, i, ps[:, i % 3, :])
                if i == 5:
                    copy_row(0)
                    split_hi(1)
            boundary(0)
            act.wait_ge(ada_rows, 2 * NC)
            load_ada(0, (0, 1), 2)
            with act.Fori(0, LOOP_Q) as q:
                mlp_quarter(0, q)
            mlp_quarter(0, LOOP_Q, last=True)
            boundary(1)
            for g in range(6):
                u = CONV_U + 2 * g
                split_hi(u + 2)
                if g in CV_GROUPS:
                    for p in (0, 1):
                        n = 2 * CV_GROUPS.index(g) + p
                        act.wait_ge(bank_done, NC + BANKS * pair(u) + 2 * p + 1)
                        if n >= 2:
                            act.wait_ge(cu_ready, n - 1)
                        nc.scalar.activation(cgate[:, p, :], ps[:, BANKS * (g % 2) + 2 * p, :], ACT.Copy).then_inc(c_copied, 1)
                        act.wait_ge(cu_ready, n + 1)
                        nc.scalar.activation(y[:, n, :], cu[:, p, 1:T + 1], ACT.Copy, scale=col(V_CONV + NC, n)).then_inc(z_mid, 1)
                else:
                    for m in range(BANKS):
                        n = BANKS * (g // 3) + m
                        act.wait_ge(gated, n + 1)
                        nc.scalar.activation(mid_hi[:, n, :], y[:, n, :], ACT.Copy).then_inc(g_hi, 1)
                split_hi(u + 3)
            for g in range(2):
                u = OUT_U + 2 * g
                split_hi(u + 2)
                for m in range(BANKS):
                    act.wait_ge(bank_done, NC + BANKS * pair(u) + m + 1)
                    finish(2, BANKS * g + m, ps[:, BANKS * g + m, :])
                if g == 0:
                    split_hi(u + 3)
            boundary(2)
            with act.Fori(0, LOOP_Q) as q:
                mlp_quarter(1, q)
            mlp_quarter(1, LOOP_Q, last=True)
            act.wait_ge(w_lo_ready, UNITS)
            for half in range(2):
                for j in range(NT):
                    act.wait_ge(x_back, half * NT + j + 1)
                    nc.scalar.activation(x_tok[:, j, half * T:(half + 1) * T], ps[:, j, :], ACT.Copy).then_inc(x_back_copied, 1)
                if half == 0:
                    root(7)

        @block.vector
        def _(dve):
            def split_lo(u, q=0):
                dve.wait_ge(w_hi_ready, q * Q_UNITS + (u + 1))
                nc.vector.tensor_tensor(w_lo[:, u % 2, :], raw[:, u % 2, :], w_hi[:, u % 2, :].bitcast(F32), ALU.subtract).then_inc(w_lo_ready, 1)

            def first_ada(a):
                s, k = a // NC, a % NC
                dve.wait_ge(ada_in[FIRST_SLOTS[a]], ada_value(a))
                if k:
                    dve.wait_ge(ada_used, a)
                    nc.vector.scalar_tensor_tensor(out=ada_sum[:, s, :], in0=ada_slot(a), scalar=silu_t[:, 3, k:k + 1],
                                                   in1=ada_sum[:, s, :], op0=ALU.mult, op1=ALU.add).then_inc(ada_used, 1)
                else:
                    nc.vector.tensor_scalar(ada_sum[:, s, :], ada_slot(a), silu_t[:, 3, 0:1], None, ALU.mult).then_inc(ada_used, 1)

            def later_ada(q, units, last):
                dve.wait_ge(sums_zero, 1)
                for i in units:
                    slots = 3 if last else 2
                    dve.wait_ge(ada_in[i % slots], (0 if last else q * (16 * LATER_SEGS)) + ada_landed(i, last))
                    dve.wait_ge(ada_used, q * ADA_Q + (ADA_DVE + i - LATER_SEGS + 1))
                    k, s = q * 2 + i // LATER_SEGS, i % LATER_SEGS
                    nc.vector.scalar_tensor_tensor(out=ada_sum[:, s, :], in0=ada_raw[:, i % slots, :], scalar=silu_t[:, 3, bass.ds(k, 1)],
                                                   in1=ada_sum[:, s, :], op0=ALU.mult, op1=ALU.add).then_inc(ada_used, 1)

            made = [0]

            def make_mod(i):
                _, layer, seg, bank = VECTORS[i]
                dve.wait_ge(ada_cols, i + 1)
                src = ps[:, bank, 0:NC]
                bias = vec[:, V_ADA_B + (layer * 6 + seg) * NC:V_ADA_B + (layer * 6 + seg + 1) * NC]
                mlp = seg >= SHIFT_F
                if seg in (SHIFT_M, SHIFT_F):
                    nc.vector.tensor_tensor(mod[:, layer, 3 * mlp + 1, :], src, bias, ALU.add).then_inc(mod_ready, 1)
                    return
                nc.vector.tensor_tensor(mod_t[:, layer, seg, :], src, bias, ALU.add).then_inc(mod_step, 1)
                made[0] += 1
                dve.wait_ge(mod_step, made[0])
                gate = seg in (GATE_M, GATE_F)
                g = V_NORM_G + (layer * 4 + 2 * mlp + gate) * NC
                nc.vector.scalar_tensor_tensor(out=mod[:, layer, 3 * mlp + 2 * gate, :], in0=mod_t[:, layer, seg, :],
                                               scalar=0.0 if gate else 1.0, in1=vec[:, g:g + NC], op0=ALU.add,
                                               op1=ALU.mult).then_inc(mod_ready, 1)

            def reciprocal_rms(k):
                rms, diag = (rms_y, diag_y) if k % 2 else (rms_x, diag_x)
                dve.wait_ge(rms_ready, k + 1)
                nc.vector.reciprocal(rms[:, 1, :], rms[:, 0, :]).then_inc(rcp_ready, 1)
                dve.wait_ge(rcp_ready, k + 1)
                if k in (0, 7):
                    return
                for j in range(NT):
                    op = nc.vector.tensor_scalar(diag[:, j, :], ident[:, :], rms[:, 1, j:j + 1], None, ALU.mult)
                op.then_inc(diag_ready, 1)

            def add_squares(n, ready, value, before):
                dve.wait_ge(ready, value)
                add_wait(dve, yy_added, before)
                nc.vector.tensor_tensor(sums[:, 0, :], sums[:, 0, :], work[:, n % 2, 0, :], ALU.add).then_inc(yy_added, 1)

            def finish(b, n):
                if n >= 1:
                    add_squares(n, y_sq, NC * b + n + 1, (NC - 1) * b + n - 1)
                if b == 3:
                    return
                to = sums if n == 0 else work[:, n % 2]
                dve.wait_ge(v_ready, NC * b + n + 1)
                nc.vector.tensor_tensor(to[:, 1, :], xs[:, n, :], y[:, n, :], ALU.mult).then_inc(xv_ready, 1)
                if n >= 1:
                    dve.wait_ge(v_sq, NC * b + n + 1)
                    dve.wait_ge(xv_ready, NC * b + n + 1)
                    add_wait(dve, xv_added, (NC - 1) * b + n - 1)
                    nc.vector.tensor_tensor(sums[:, 1:3, :], sums[:, 1:3, :], work[:, n % 2, 1:3, :], ALU.add).then_inc(xv_added, 1)

            def new_xx(b):
                r = rms_y[:, 1, :]
                dve.wait_ge(xv_cols, b + 1)
                nc.vector.tensor_tensor(xx_t[:, 0, :], ps[:, XV_BANK[b], NT:2 * NT], r, ALU.mult).then_inc(xx_step, 1)
                dve.wait_ge(xx_step, 4 * b + 1)
                nc.vector.scalar_tensor_tensor(out=xx_t[:, 1, :], in0=ps[:, XV_BANK[b], 0:NT], scalar=2.0, in1=xx_t[:, 0, :],
                                               op0=ALU.mult, op1=ALU.add).then_inc(xx_step, 1)
                dve.wait_ge(xx_step, 4 * b + 2)
                nc.vector.tensor_tensor(xx_t[:, 2, :], xx_t[:, 1, :], r, ALU.mult).then_inc(xx_step, 1)
                dve.wait_ge(xx_step, 4 * b + 3)
                nc.vector.tensor_tensor(xx_t[:, 3, :], xx_t[:, 2, :], xx[:, :], ALU.add).then_inc(xx_step, 1)
                dve.wait_ge(xx_step, 4 * b + 4)
                nc.vector.tensor_scalar(xx[:, :], xx_t[:, 3, :], 0.0, None, ALU.max).then_inc(xx_ready, 1)

            def boundary(b):
                first, second, third = AT_BOUNDARY[b]
                if b > 0:
                    make_mod(first)
                    make_mod(second)
                    make_mod(third)
                reciprocal_rms(2 * b + 1)
                new_xx(b)
                reciprocal_rms(2 * b + 2)
                if b == 0:
                    make_mod(first)
                dve.wait_ge(bcast_done, 2 * b + 1)
                def normed(n):
                    nc.vector.tensor_tensor(y[:, n, :], y[:, n, :], ps[:, R_BANK, :], ALU.mult).then_inc(y_norm, 1)

                def low(n):
                    dve.wait_ge(h_hi, NC * (b + 1) + n + 1)
                    nc.vector.tensor_tensor(in_lo[:, n, :], y[:, n, :], in_hi[:, n, :].bitcast(F32), ALU.subtract).then_inc(h_lo, 1)

                normed(0)
                for n in range(NC):
                    dve.wait_ge(y_norm, NC * b + n + 1)
                    nc.vector.tensor_tensor(xs[:, n, :], xs[:, n, :], y[:, n, :], ALU.add).then_inc(x_new, 1)
                    if n + 1 < NC:
                        normed(n + 1)
                    if n == 0:
                        dve.wait_ge(bcast_done, 2 * b + 2)
                    dve.wait_ge(x_new, NC * b + n + 1)
                    nc.vector.tensor_tensor(y[:, n, :], xs[:, n, :], ps[:, R2_BANK, :], ALU.mult).then_inc(h_norm, 1)
                    if b == 0 and n == 0:
                        make_mod(second)
                    if n > 0:
                        low(n - 1)
                    if n in ((0, 6) if b == 0 else (4,)):
                        dve.wait_ge(w_lo_by_pool, b + 1 + (b > 0 or n == 6))
                        nc.vector.tensor_copy(note[:, 1:2], note[:, 0:1]).then_inc(w_lo_ready, 1)
                low(NC - 1)
            def result():
                reciprocal_rms(7)
                for half in range(2):
                    for j in range(NT):
                        dve.wait_ge(out_turned, half * NT + j + 1)
                        dve.wait_ge(x_back_copied, half * NT + j + 1)
                        rows = x_tok[:, j, half * T:(half + 1) * T]
                        nc.vector.scalar_tensor_tensor(out=rows, in0=ps[:, NT + j, :], scalar=rms_y[:, 1, j:j + 1], in1=rows, op0=ALU.mult, op1=ALU.add).then_inc(out_made, 1)

            def hidden(layer, q, j):
                for m in range(BANKS):
                    n = BANKS * (j // 2) + m
                    i = layer * QUARTERS * NC + n
                    dve.wait_ge(hid_hi, q * NC + (i + 1))
                    nc.vector.tensor_tensor(relu[:, n % 2, :], relu[:, n % 2, :], relu[:, n % 2, :], ALU.mult).then_inc(hid_sq, 1)
                    dve.wait_ge(hid_sq, q * NC + (i + 1))
                    nc.vector.tensor_tensor(mid_lo[:, n, :], relu[:, n % 2, :], mid_hi[:, n, :].bitcast(F32), ALU.subtract).then_inc(hid_lo, 1)

            def mlp_quarter(layer, q, last=False):
                b = 1 + 2 * layer
                for j in range(Q_UNITS):
                    u = FFN_U[layer] + j
                    if j == 3:
                        hidden(layer, q, j)
                    if j in (5, 7):
                        dve.wait_ge(y_zero, layer + 1)
                        for m in range(BANKS):
                            n = BANKS * (j // 2 - 2) + m
                            dve.wait_ge(bank_done, q * (BANKS * Q_UNITS // 2) + (NC + BANKS * pair(u) + m + 1))
                            nc.vector.tensor_tensor(y[:, n, :], y[:, n, :], ps[:, BANKS * (j // 2 - 2) + m, :], ALU.add).then_inc(y_sum, 1)
                            if last and n > 4:
                                finish(b, n - 1)
                    if last and j == 7:
                        finish(b, NC - 1)
                    elif not (last and u + Q_UNITS * q + 2 >= UNITS):
                        split_lo(u + 2, q)
                    if j == 1:
                        hidden(layer, q, j)
                    if last and j == 5:
                        if layer == 0:
                            make_mod(5)
                        for n in range(4):
                            finish(b, n)
                    if layer == 0:
                        if last and LAST_STEPS[j]:
                            later_ada(q, last_units(j), True)
                        elif not last and j < LATER_SEGS:
                            later_ada(q, (2 * j, 2 * j + 1), False)

            nc.vector.memset(note[:, :], 0.0)
            dve.wait_ge(exp_ready, 1)
            nc.vector.tensor_scalar(silu_t[:, 1, :], silu_t[:, 0, :], 1.0, None, ALU.add).then_inc(silu_step, 1)
            dve.wait_ge(silu_step, 1)
            nc.vector.reciprocal(silu_t[:, 2, :], silu_t[:, 1, :]).then_inc(silu_step, 1)
            dve.wait_ge(silu_step, 2)
            nc.vector.tensor_tensor(silu_t[:, 3, :], silu_t[:, 2, :], vec[:, V_C:V_END], ALU.mult).then_inc(silu_step, 1)
            dve.wait_ge(silu_step, 3)

            reciprocal_rms(0)
            for j in range(NT):
                dve.wait_ge(x_in[j], 16)
                nc.vector.tensor_scalar(xn_tok[:, j, :], x_tok[:, j, :], rms_x[:, 1, j:j + 1], None, ALU.mult).then_inc(xn_ready, 1)
            for a in range(2 * NC):
                first_ada(a)
            make_mod(0)
            make_mod(1)
            dve.wait_ge(mod_ready, 2)
            for g, w in enumerate(WINDOWS):
                op = nc.vector.tensor_scalar(a_by_w[:, 2 * g:2 * g + 2], mod[:, 0, 0, 2 * g:2 * g + 2], 1.0 / w, None, ALU.mult)
            op.then_inc(mean_scale, 1)
            split_lo(POOL_U)
            for i in range(NC + 2):
                if 1 <= i <= NC:
                    n = i - 1
                    dve.wait_ge(pool_h, i)
                    nc.vector.tensor_tensor(y[:, n, :], y[:, n, :], h_pool[:, n % 2, :], ALU.subtract).then_inc(pool_diff, 1)
                if i >= 2:
                    n = i - 2
                    dve.wait_ge(h_hi, i - 1)
                    nc.vector.tensor_tensor(in_lo[:, n, :], y[:, n, :], in_hi[:, n, :].bitcast(F32), ALU.subtract).then_inc(h_lo, 1)
                if i < NC:
                    first_ada(2 * NC + i)
            make_mod(2)
            dve.wait_ge(mod_ready, 3)
            nc.vector.tensor_tensor(pool_gate[:, :], mod[:, 0, 2, :], vec[:, V_POOL:V_CONV], ALU.mult).then_inc(pool_gate_ready, 1)
            for n in range(NC):
                finish(0, n)
            boundary(0)
            with dve.Fori(0, LOOP_Q) as q:
                mlp_quarter(0, q)
            mlp_quarter(0, LOOP_Q, last=True)
            boundary(1)
            dve.wait_ge(cu_pad, 1)
            for g in range(6):
                u = CONV_U + 2 * g
                split_lo(u + 2)
                if g in CV_GROUPS:
                    for p in (0, 1):
                        n = 2 * CV_GROUPS.index(g) + p
                        dve.wait_ge(bank_done, NC + BANKS * pair(u) + 2 * p + 2)
                        dve.wait_ge(c_copied, n + 1)
                        nc.vector.tensor_tensor(cu[:, p, 1:T + 1], cgate[:, p, :], ps[:, BANKS * (g % 2) + 2 * p + 1, :], ALU.mult).then_inc(cu_ready, 1)
                        dve.wait_ge(z_mid, n + 1)
                        nc.vector.scalar_tensor_tensor(out=y[:, n, :], in0=cu[:, p, 0:T], scalar=col(V_CONV, n), in1=y[:, n, :],
                                                       op0=ALU.mult, op1=ALU.add).then_inc(z_left, 1)
                        dve.wait_ge(z_left, n + 1)
                        nc.vector.scalar_tensor_tensor(out=y[:, n, :], in0=cu[:, p, 2:T + 2], scalar=col(V_CONV + 2 * NC, n), in1=y[:, n, :],
                                                       op0=ALU.mult, op1=ALU.add).then_inc(z_ready, 1)
                else:
                    for m in range(BANKS):
                        n = BANKS * (g // 3) + m
                        dve.wait_ge(bank_done, NC + BANKS * pair(u) + m + 1)
                        dve.wait_ge(z_ready, n + 1)
                        nc.vector.tensor_tensor(y[:, n, :], y[:, n, :], ps[:, BANKS * (g % 2) + m, :], ALU.mult).then_inc(gated, 1)
                        dve.wait_ge(g_hi, n + 1)
                        nc.vector.tensor_tensor(mid_lo[:, n, :], y[:, n, :], mid_hi[:, n, :].bitcast(F32), ALU.subtract).then_inc(g_lo, 1)
                split_lo(u + 3)
            for g in range(2):
                u = OUT_U + 2 * g
                split_lo(u + 2)
                for m in range(BANKS):
                    finish(2, BANKS * g + m)
                if g == 0:
                    split_lo(u + 3)
            boundary(2)
            with dve.Fori(0, LOOP_Q) as q:
                mlp_quarter(1, q)
            mlp_quarter(1, LOOP_Q, last=True)
            result()

        @block.gpsimd
        def _(pool):
            nc.gpsimd.memset(ident[:, :], 0.0).then_inc(ident_zero, 1)
            nc.gpsimd.memset(ones[:, :], 1.0).then_inc(consts_ready, 1)
            pool.wait_ge(ident_zero, 1)
            nc.gpsimd.affine_select(out=ident[:, :], in_=ident[:, :], compare_op=ALU.not_equal, fill=1.0, base=0,
                                    pattern=[[-1, P]], channel_multiplier=1).then_inc(consts_ready, 1)
            nc.gpsimd.memset(eps[:, :], EPS).then_inc(eps_ready, 1)
            steps = [0]

            def step(op):
                steps[0] += 1
                op.then_inc(bands_step, 1)
                pool.wait_ge(bands_step, steps[0])

            def split_lo(u):
                pool.wait_ge(w_hi_ready, u + 1)
                nc.gpsimd.tensor_tensor(w_lo[:, u % 2, :], raw[:, u % 2, :], w_hi[:, u % 2, :].bitcast(F32), ALU.subtract).then_inc(w_lo_by_pool, 1)

            step(nc.gpsimd.memset(sums[:, :, :], 1.0))
            for g, w in enumerate(WINDOWS):
                op = nc.gpsimd.affine_select(out=bands[:, g, :], in_=bands[:, g, :], compare_op=ALU.is_ge, fill=0.0,
                                             base=w // 2 - 1 - P, pattern=[[1, 3 * P]], channel_multiplier=-1)
            step(op)
            for g, w in enumerate(WINDOWS):
                op = nc.gpsimd.affine_select(out=bands[:, g, :], in_=bands[:, g, :], compare_op=ALU.is_ge, fill=0.0,
                                             base=w // 2 + P, pattern=[[-1, 3 * P]], channel_multiplier=1)
            step(op)
            for e in range(2):
                op = nc.gpsimd.tensor_copy(ends[e], bands[:, :, P:2 * P])
            step(op)
            for g, w in enumerate(WINDOWS):
                half = w // 2
                for e, t, n in [(0, t, t + half) for t in range(half)] + [(1, P - half + 1 + r, w - 1 - r) for r in range(half - 1)]:
                    op = nc.gpsimd.tensor_scalar(ends[e][:, g, t:t + 1], bands[:, g, P + t:P + t + 1], w / n, None, ALU.mult)
            op.then_inc(bands_ready, 1)
            split_lo(1)
            split_lo(2)
            pool.wait_ge(ada_cols, len(FIRST_SEGS))
            nc.gpsimd.memset(ada_sum[:, :, :], 0.0).then_inc(sums_zero, 1)
            pool.wait_ge(h_lo, 2 * NC)
            nc.gpsimd.memset(y[:, :, :], 0.0).then_inc(y_zero, 1)
            pool.wait_ge(ada_cols, 8)
            nc.gpsimd.memset(cu[:, :, 0:1], 0.0)
            nc.gpsimd.memset(cu[:, :, T + 1:T + 2], 0.0).then_inc(cu_pad, 1)
            split_lo(SECOND[1])
            split_lo(SECOND[2])
            pool.wait_ge(h_lo, 4 * NC)
            nc.gpsimd.memset(y[:, :, :], 0.0).then_inc(y_zero, 1)


_INS = ['x', 'c', 'ada_w', 'ada_b', 'norm_g', 'ffn_w1', 'ffn_w2', 'pool_w', 'pool_scale', 'conv_in_w', 'conv_w', 'conv_out_w']


def kernel(**inputs):
    import numpy as _np
    import concourse.bacc as _bacc
    from concourse import mybir as _mybir
    from concourse.bass_utils import run_bass_kernel_spmd as _run

    nc = _bacc.Bacc("TRN2", target_bir_lowering=False, num_devices=1)
    arrays, args = {}, []
    for name in _INS:
        a = _np.ascontiguousarray(inputs[name])
        arrays[f"in_{name}_dram"] = a
        args.append(nc.dram_tensor(f"in_{name}_dram", a.shape, _mybir.dt.from_np(a.dtype), kind="ExternalInput").ap())
    args.append(nc.dram_tensor("out_dram", (1, T, D), _mybir.dt.float32, kind="ExternalOutput").ap())
    trunk(nc, *args)
    r = _run(nc, [arrays], core_ids=[0])
    return r.results[0]["out_dram"]
```
